# Optimizing a Trainium2 kernel written in Bass

```python
import jax, jax.numpy as jnp
from jax import lax
import numpy as np

D_MODEL = 1024
BATCH = 1
SEQ = 256
DEPTH = 2

CHUNK = 64
Q_BLOCK = 128
PLE_DIM = 256
D_FF = 2816
CONV_DIM = 512
CONV_GROUPS = 8
CONV_K = 3
N_HEADS = 8
NOPE_DIM = 128
ROPE_DIM = 64
V_DIM = 128
Q_LORA = 384
KV_LORA = 256
ROPE_THETA = 10000.0
EPS = 1e-6
QK_DIM = NOPE_DIM + ROPE_DIM
ATTN_SCALE = QK_DIM ** -0.5
IN_SPLITS = (CONV_DIM, CONV_DIM, CONV_DIM, Q_LORA, KV_LORA, ROPE_DIM, D_MODEL, D_MODEL)
IN_COLS = sum(IN_SPLITS)


def rmsnorm(x, g):
    xf = x.astype(jnp.float32)
    y = xf * lax.rsqrt(jnp.mean(xf * xf, axis=-1, keepdims=True) + EPS)
    return (y * g.astype(jnp.float32)).astype(x.dtype)

def swiglu(x, w_gu, w_down):
    g, u = jnp.split(x @ w_gu, 2, axis=-1)
    return (jax.nn.silu(g) * u) @ w_down

def rope_tables(positions):
    inv_freq = ROPE_THETA ** (-jnp.arange(0, ROPE_DIM, 2, dtype=jnp.float32) / ROPE_DIM)
    ang = positions.astype(jnp.float32)[..., None] * inv_freq
    return jnp.cos(ang), jnp.sin(ang)

def apply_rope(x, cos, sin):
    half = ROPE_DIM // 2
    xf = x.astype(jnp.float32)
    x1, x2 = xf[..., :half], xf[..., half:]
    return jnp.concatenate([x1 * cos - x2 * sin, x2 * cos + x1 * sin], axis=-1).astype(x.dtype)

def short_conv_branch(b_gate, c_gate, v, conv_w, w_conv_out):
    seq = v.shape[1]
    z = c_gate * v
    zp = jnp.pad(z, ((0, 0), (CONV_K - 1, 0), (0, 0)))
    y = conv_w[0] * zp[:, 0:seq]
    for j in range(1, CONV_K):
        y = y + conv_w[j] * zp[:, j:j + seq]
    return (b_gate * y) @ w_conv_out

def block_causal_attention(q_nope, q_rope, k_nope, k_rope, v):
    seq = q_nope.shape[1]
    outs = []
    for i in range(seq // Q_BLOCK):
        q0, q1 = i * Q_BLOCK, (i + 1) * Q_BLOCK
        kn, kr, vb = k_nope[:, :q1], k_rope[:, :q1], v[:, :q1]
        s = (jnp.einsum('bqhd,bkhd->bhqk', q_nope[:, q0:q1], kn)
             + jnp.einsum('bqhd,bkd->bhqk', q_rope[:, q0:q1], kr)).astype(jnp.float32) * ATTN_SCALE
        q_chunk = (q0 + jnp.arange(Q_BLOCK)) // CHUNK
        k_chunk = jnp.arange(q1) // CHUNK
        mask = k_chunk[None, :] <= q_chunk[:, None]
        s = jnp.where(mask, s, -1e30)
        pr = jax.nn.softmax(s, axis=-1).astype(v.dtype)
        outs.append(jnp.einsum('bhqk,bkhd->bqhd', pr, vb))
    return jnp.concatenate(outs, axis=1)

def mla_branch(q_c, kv_c, k_r, q_norm_g, kv_norm_g, w_uq, w_ukv, w_mla_out, cos, sin):
    b, s, _ = q_c.shape
    q = (rmsnorm(q_c, q_norm_g) @ w_uq).reshape(b, s, N_HEADS, QK_DIM)
    q_nope = q[..., :NOPE_DIM]
    q_rope = apply_rope(q[..., NOPE_DIM:], cos[:, :, None, :], sin[:, :, None, :])
    kv = (rmsnorm(kv_c, kv_norm_g) @ w_ukv).reshape(b, s, N_HEADS, NOPE_DIM + V_DIM)
    k_nope, v = kv[..., :NOPE_DIM], kv[..., NOPE_DIM:]
    k_rope = apply_rope(k_r, cos, sin)
    o = block_causal_attention(q_nope, q_rope, k_nope, k_rope, v)
    return o.reshape(b, s, N_HEADS * V_DIM) @ w_mla_out

def first_inputs(seed: int = 0) -> dict:
    key = jax.random.key(seed)
    ks = jax.random.split(key, 24)
    f32 = jnp.float32

    def w(k, shape, fan_in):
        return jax.random.normal(k, shape, f32) * (fan_in ** -0.5)

    def gain(k, shape):
        return 1.0 + 0.05 * jax.random.normal(k, shape, f32)

    x = jax.random.normal(ks[0], (BATCH, SEQ, D_MODEL), f32)
    p = jax.random.normal(ks[1], (DEPTH, BATCH, SEQ, PLE_DIM), f32)
    offset = jax.random.randint(ks[2], (BATCH, 1), 0, 4096, dtype=jnp.int32)
    positions = offset + jnp.arange(SEQ, dtype=jnp.int32)[None, :]
    return {
        "x": x,
        "p": p,
        "positions": positions,
        "ffn1_norm": gain(ks[3], (DEPTH, D_MODEL)),
        "ffn1_w_gu": w(ks[4], (DEPTH, D_MODEL, 2 * D_FF), D_MODEL),
        "ffn1_w_down": w(ks[5], (DEPTH, D_FF, D_MODEL), D_FF),
        "mix_norm": gain(ks[6], (DEPTH, D_MODEL)),
        "w_in": w(ks[7], (DEPTH, D_MODEL, IN_COLS), D_MODEL),
        "conv_w": w(ks[8], (DEPTH, CONV_K, CONV_DIM), CONV_K),
        "w_conv_out": w(ks[9], (DEPTH, CONV_DIM, D_MODEL), CONV_DIM),
        "q_norm": gain(ks[10], (DEPTH, Q_LORA)),
        "kv_norm": gain(ks[11], (DEPTH, KV_LORA)),
        "w_uq": w(ks[12], (DEPTH, Q_LORA, N_HEADS * QK_DIM), Q_LORA),
        "w_ukv": w(ks[13], (DEPTH, KV_LORA, N_HEADS * (NOPE_DIM + V_DIM)), KV_LORA),
        "w_mla_out": w(ks[14], (DEPTH, N_HEADS * V_DIM, D_MODEL), N_HEADS * V_DIM),
        "w_o": w(ks[15], (DEPTH, D_MODEL, D_MODEL), D_MODEL),
        "ffn2_norm": gain(ks[16], (DEPTH, D_MODEL)),
        "ffn2_w_gu": w(ks[17], (DEPTH, D_MODEL, 2 * D_FF), D_MODEL),
        "ffn2_w_down": w(ks[18], (DEPTH, D_FF, D_MODEL), D_FF),
        "ple_norm": gain(ks[19], (DEPTH, D_MODEL)),
        "w_ple_gate": w(ks[20], (DEPTH, D_MODEL, D_MODEL), D_MODEL),
        "w_ple_proj": w(ks[21], (DEPTH, PLE_DIM, D_MODEL), PLE_DIM),
        "final_norm": gain(ks[22], (D_MODEL,)),
    }

def first_block(x, p, positions, ffn1_norm, ffn1_w_gu, ffn1_w_down, mix_norm, w_in, conv_w,
              w_conv_out, q_norm, kv_norm, w_uq, w_ukv, w_mla_out, w_o, ffn2_norm, ffn2_w_gu,
              ffn2_w_down, ple_norm, w_ple_gate, w_ple_proj, final_norm):
    cos, sin = rope_tables(positions)
    split_pts = list(np.cumsum(IN_SPLITS)[:-1])
    h = x
    for i in range(DEPTH):
        h = h + 0.5 * swiglu(rmsnorm(h, ffn1_norm[i]), ffn1_w_gu[i], ffn1_w_down[i])

        u = rmsnorm(h, mix_norm[i])
        b_g, c_g, v_c, q_c, kv_c, k_r, g_conv, g_mla = jnp.split(u @ w_in[i], split_pts, axis=-1)
        y_conv = short_conv_branch(b_g, c_g, v_c, conv_w[i], w_conv_out[i])
        y_mla = mla_branch(q_c, kv_c, k_r, q_norm[i], kv_norm[i], w_uq[i], w_ukv[i],
                           w_mla_out[i], cos, sin)
        merged = jax.nn.sigmoid(g_conv) * y_conv + jax.nn.sigmoid(g_mla) * y_mla
        h = h + merged @ w_o[i]

        h = h + 0.5 * swiglu(rmsnorm(h, ffn2_norm[i]), ffn2_w_gu[i], ffn2_w_down[i])

        gate = jax.nn.sigmoid(rmsnorm(h, ple_norm[i]) @ w_ple_gate[i])
        h = h + gate * (p[i] @ w_ple_proj[i])
    return rmsnorm(h, final_norm)


GLA_HEADS = 4
GLA_DK = D_MODEL // 2 // GLA_HEADS
GLA_DV = D_MODEL // GLA_HEADS
GLA_GATE_RANK = 16
GLA_TAU = 16.0
GLA_CHUNK = 64

NSA_HEADS = 16
NSA_GROUPS = 4
NSA_HPG = NSA_HEADS // NSA_GROUPS
NSA_HEAD_DIM = D_MODEL // NSA_HEADS
CMP_BLOCK = 32
CMP_STRIDE = 16
CMP_HIDDEN = 256
SLC_BLOCK = 64
SLC_TOP_N = 16
WINDOW = 512

ROPE_THETA_2 = 500000.0
ROT_DIM = NSA_HEAD_DIM // 4

N_EXPERTS = 16
N_EXPERT_GROUPS = 4
EXPERTS_PER_GROUP = N_EXPERTS // N_EXPERT_GROUPS
TOP_K = 2
D_FF_EXPERT = D_MODEL // 4

DN_ALPHA = (2 * DEPTH) ** 0.25
DN_BETA = (8 * DEPTH) ** -0.25
LN_EPS = 1e-5
NEG = -1e30
BIG = 1e30

N_GLA_LAYERS = (DEPTH + 1) // 2
N_NSA_LAYERS = DEPTH // 2
GLA_IN = 2 * GLA_HEADS * GLA_DK + 2 * GLA_HEADS * GLA_DV + GLA_GATE_RANK
NSA_IN = NSA_HEADS * NSA_HEAD_DIM + 6 * NSA_GROUPS * NSA_HEAD_DIM + 3 * NSA_HEADS


def layer_norm(x, g, b):
    xf = x.astype(jnp.float32)
    mu = jnp.mean(xf, axis=-1, keepdims=True)
    var = jnp.mean(jnp.square(xf - mu), axis=-1, keepdims=True)
    y = (xf - mu) * lax.rsqrt(var + LN_EPS) * g.astype(jnp.float32) + b.astype(jnp.float32)
    return y.astype(x.dtype)

def partial_rope(t, pos):
    half = ROT_DIM // 2
    inv_freq = jnp.power(ROPE_THETA_2, -jnp.arange(half, dtype=jnp.float32) * (2.0 / ROT_DIM))
    ang = pos.astype(jnp.float32)[:, None] * inv_freq[None, :]
    cos = jnp.cos(ang).astype(t.dtype)
    sin = jnp.sin(ang).astype(t.dtype)
    x1 = t[..., :half]
    x2 = t[..., half:ROT_DIM]
    return jnp.concatenate([x1 * cos - x2 * sin, x2 * cos + x1 * sin, t[..., ROT_DIM:]], axis=-1)

def masked_softmax(scores, mask):
    return jax.nn.softmax(jnp.where(mask, scores.astype(jnp.float32), NEG), axis=-1)

def gla_mixer(x, w_in, w_gate_up, b_gate, norm_g, w_out):
    B, S, _ = x.shape
    H, DK, DV, C = GLA_HEADS, GLA_DK, GLA_DV, GLA_CHUNK
    N = S // C
    f32 = jnp.float32
    proj = x @ w_in
    cuts = np.cumsum([H * DK, H * DK, H * DV, GLA_GATE_RANK]).tolist()
    q, k, v, g_low, r = jnp.split(proj, cuts, axis=-1)
    log_a = jax.nn.log_sigmoid((g_low @ w_gate_up + b_gate).astype(f32)) / GLA_TAU

    def chunks(t, d):
        return t.reshape(B, N, C, H, d).transpose(0, 3, 1, 2, 4).astype(f32)

    q = chunks(q, DK) * (DK ** -0.5)
    k = chunks(k, DK)
    v = chunks(v, DV)
    b = jnp.cumsum(chunks(log_a, DK), axis=3)
    b_last = b[:, :, :, -1:, :]
    q_dec = q * jnp.exp(b)
    causal = jnp.tril(jnp.ones((C, C), dtype=bool))
    scores = jnp.einsum('bhnid,bhnjd->bhnij', q_dec, k * jnp.exp(-b))
    o_intra = jnp.einsum('bhnij,bhnjv->bhniv', jnp.where(causal, scores, 0.0), v)
    kv = jnp.einsum('bhncd,bhncv->bhndv', k * jnp.exp(b_last - b), v)
    decay = jnp.exp(b_last[:, :, :, 0, :])

    def step(state, inp):
        dec, kv_n = inp
        return dec[..., None] * state + kv_n, state

    _, states = lax.scan(step, jnp.zeros((B, H, DK, DV), f32),
                         (jnp.moveaxis(decay, 2, 0), jnp.moveaxis(kv, 2, 0)))
    o_inter = jnp.einsum('bhncd,nbhdv->bhncv', q_dec, states)
    o = (o_intra + o_inter).transpose(0, 2, 3, 1, 4).reshape(B, S, H, DV)
    o = o * lax.rsqrt(jnp.mean(jnp.square(o), axis=-1, keepdims=True) + LN_EPS) * norm_g.astype(f32)
    o = o.reshape(B, S, H * DV) * jax.nn.silu(r.astype(f32))
    return o.astype(x.dtype) @ w_out

def compress(t, w1, w2, pe):
    B, G, S, Dh = t.shape
    n_chunk = S // CMP_STRIDE
    span = CMP_BLOCK // CMP_STRIDE
    nc = n_chunk - span + 1
    ch = t.reshape(B, G, n_chunk, CMP_STRIDE, Dh)
    blocks = jnp.concatenate([ch[:, :, i:i + nc] for i in range(span)], axis=3)
    blocks = (blocks + pe).reshape(B, G, nc, CMP_BLOCK * Dh)
    return jax.nn.silu(blocks @ w1) @ w2

def nsa_mixer(x, w_in, w_ck1, w_ck2, w_cv1, w_cv2, cmp_pe, w_out):
    B, S, _ = x.shape
    H, G, HPG, Dh = NSA_HEADS, NSA_GROUPS, NSA_HPG, NSA_HEAD_DIM
    f32 = jnp.float32
    proj = x @ w_in
    cuts = np.cumsum([H * Dh] + [G * Dh] * 6).tolist()
    q, kc, vc, ks, vs, kw, vw, gates = jnp.split(proj, cuts, axis=-1)
    pos = jnp.arange(S, dtype=jnp.int32)

    def kv_heads(t):
        return t.reshape(B, S, G, Dh).transpose(0, 2, 1, 3)

    q = partial_rope(q.reshape(B, S, G, HPG, Dh).transpose(0, 2, 3, 1, 4), pos) * (Dh ** -0.5)
    gates = jax.nn.sigmoid(gates.astype(f32)).reshape(B, S, G, HPG, 3).transpose(0, 2, 3, 1, 4)

    span = CMP_BLOCK // CMP_STRIDE
    nc = S // CMP_STRIDE - span + 1
    cmp_end = jnp.arange(nc, dtype=jnp.int32) * CMP_STRIDE + (CMP_BLOCK - 1)
    k_cmp = partial_rope(compress(kv_heads(kc), w_ck1, w_ck2, cmp_pe), cmp_end)
    v_cmp = compress(kv_heads(vc), w_cv1, w_cv2, cmp_pe).astype(f32)

    ns = S // SLC_BLOCK
    n_sel = min(SLC_TOP_N, ns)
    k_slc = partial_rope(kv_heads(ks), pos).reshape(B, G, ns, SLC_BLOCK, Dh)
    v_slc = kv_heads(vs).reshape(B, G, ns, SLC_BLOCK, Dh)
    ratio = SLC_BLOCK // CMP_STRIDE
    pad_amt = ratio * ns + span - 1 - nc

    pad = ((0, 0), (0, 0), (WINDOW, 0), (0, 0))
    k_win = jnp.pad(partial_rope(kv_heads(kw), pos), pad)
    v_win = jnp.pad(kv_heads(vw), pad)

    bi = jnp.arange(B)[:, None, None, None]
    gi = jnp.arange(G)[None, :, None, None]
    blk_ids = jnp.arange(ns)
    in_blk = jnp.arange(SLC_BLOCK)
    win_off = jnp.arange(WINDOW + Q_BLOCK) - WINDOW

    def query_block(qi):
        s0 = qi * Q_BLOCK
        qpos = s0 + jnp.arange(Q_BLOCK)
        qb = lax.dynamic_slice_in_dim(q, s0, Q_BLOCK, axis=3)
        gb = lax.dynamic_slice_in_dim(gates, s0, Q_BLOCK, axis=3)

        cmask = cmp_end[None, :] <= qpos[:, None]
        p_cmp = masked_softmax(jnp.einsum('bghqd,bgcd->bghqc', qb, k_cmp), cmask)
        p_cmp = p_cmp * jnp.any(cmask, axis=-1)[:, None]
        o_cmp = jnp.einsum('bghqc,bgcd->bghqd', p_cmp, v_cmp)

        p_grp = jnp.pad(p_cmp.sum(axis=2), ((0, 0), (0, 0), (0, 0), (0, pad_amt)))
        imp = p_grp[..., 0:ratio * ns:ratio]
        for m in range(ratio):
            for n in range(span):
                if m + n > 0:
                    imp = imp + p_grp[..., m + n:m + n + ratio * ns:ratio]
        cur = (qpos // SLC_BLOCK)[:, None]
        forced = (blk_ids == 0) | (blk_ids == cur) | (blk_ids == cur - 1)
        imp = jnp.where(blk_ids <= cur, jnp.where(forced, BIG, imp), NEG)
        _, sel = lax.top_k(imp, n_sel)
        k_sel = k_slc[bi, gi, sel].reshape(B, G, Q_BLOCK, n_sel * SLC_BLOCK, Dh)
        v_sel = v_slc[bi, gi, sel].reshape(B, G, Q_BLOCK, n_sel * SLC_BLOCK, Dh)
        kpos = (sel[..., None] * SLC_BLOCK + in_blk).reshape(B, G, Q_BLOCK, n_sel * SLC_BLOCK)
        smask = (kpos <= qpos[:, None])[:, :, None]
        p_slc = masked_softmax(jnp.einsum('bghqd,bgqkd->bghqk', qb, k_sel), smask)
        o_slc = jnp.einsum('bghqk,bgqkd->bghqd', p_slc, v_sel.astype(f32))

        kw_b = lax.dynamic_slice_in_dim(k_win, s0, WINDOW + Q_BLOCK, axis=2)
        vw_b = lax.dynamic_slice_in_dim(v_win, s0, WINDOW + Q_BLOCK, axis=2)
        kwpos = s0 + win_off
        rel = qpos[:, None] - kwpos[None, :]
        wmask = (rel >= 0) & (rel < WINDOW) & (kwpos[None, :] >= 0)
        p_win = masked_softmax(jnp.einsum('bghqd,bgkd->bghqk', qb, kw_b), wmask)
        o_win = jnp.einsum('bghqk,bgkd->bghqd', p_win, vw_b.astype(f32))

        o = gb[..., 0:1] * o_cmp + gb[..., 1:2] * o_slc + gb[..., 2:3] * o_win
        return o.astype(x.dtype)

    outs = lax.map(query_block, jnp.arange(S // Q_BLOCK))
    o = outs.transpose(1, 0, 4, 2, 3, 5).reshape(B, S, H * Dh)
    return o @ w_out

def moe_ffn(x, w_router, b_router, w_gate, w_up, w_down):
    B, S, D = x.shape
    xt = x.reshape(B * S, D)
    n = xt.shape[0]
    s = jax.nn.sigmoid((xt @ w_router).astype(jnp.float32))
    biased = s + b_router.astype(jnp.float32)
    grp_score = lax.top_k(biased.reshape(n, N_EXPERT_GROUPS, EXPERTS_PER_GROUP), TOP_K)[0].sum(-1)
    grp = jnp.argmax(grp_score, axis=-1)
    in_grp = (jnp.arange(N_EXPERTS) // EXPERTS_PER_GROUP)[None, :] == grp[:, None]
    _, top_e = lax.top_k(jnp.where(in_grp, biased, NEG), TOP_K)
    w = jnp.take_along_axis(s, top_e, axis=-1)
    w = w / jnp.sum(w, axis=-1, keepdims=True)
    gate = jnp.zeros((n, N_EXPERTS), jnp.float32).at[jnp.arange(n)[:, None], top_e].set(w)
    h = jax.nn.silu(jnp.einsum('nd,edf->nef', xt, w_gate)) * jnp.einsum('nd,edf->nef', xt, w_up)
    h = h * gate[:, :, None].astype(h.dtype)
    return jnp.einsum('nef,efd->nd', h, w_down).reshape(B, S, D)

def second_inputs(seed: int = 0) -> dict:
    key = jax.random.key(seed)
    ks = jax.random.split(key, 20)
    f32 = jnp.float32

    def nrm(k, shape, scale):
        return jax.random.normal(k, shape, f32) * scale

    D = D_MODEL
    nG, nN = N_GLA_LAYERS, N_NSA_LAYERS
    cmp_in = CMP_BLOCK * NSA_HEAD_DIM
    return {
        'x': nrm(ks[0], (BATCH, SEQ, D), 1.0),
        'gla_w_in': nrm(ks[1], (nG, D, GLA_IN), D ** -0.5),
        'gla_w_gate_up': nrm(ks[2], (nG, GLA_GATE_RANK, GLA_HEADS * GLA_DK), GLA_GATE_RANK ** -0.5),
        'gla_b_gate': nrm(ks[3], (nG, GLA_HEADS * GLA_DK), 0.1),
        'gla_norm_g': 1.0 + nrm(ks[4], (nG, GLA_DV), 0.02),
        'gla_w_out': nrm(ks[5], (nG, GLA_HEADS * GLA_DV, D), DN_BETA * (GLA_HEADS * GLA_DV) ** -0.5),
        'nsa_w_in': nrm(ks[6], (nN, D, NSA_IN), D ** -0.5),
        'nsa_w_cmp_k1': nrm(ks[7], (nN, cmp_in, CMP_HIDDEN), cmp_in ** -0.5),
        'nsa_w_cmp_k2': nrm(ks[8], (nN, CMP_HIDDEN, NSA_HEAD_DIM), CMP_HIDDEN ** -0.5),
        'nsa_w_cmp_v1': nrm(ks[9], (nN, cmp_in, CMP_HIDDEN), cmp_in ** -0.5),
        'nsa_w_cmp_v2': nrm(ks[10], (nN, CMP_HIDDEN, NSA_HEAD_DIM), CMP_HIDDEN ** -0.5),
        'nsa_cmp_pe': nrm(ks[11], (nN, CMP_BLOCK, NSA_HEAD_DIM), 0.1),
        'nsa_w_out': nrm(ks[12], (nN, NSA_HEADS * NSA_HEAD_DIM, D), DN_BETA * (NSA_HEADS * NSA_HEAD_DIM) ** -0.5),
        'moe_w_router': nrm(ks[13], (D, N_EXPERTS), D ** -0.5),
        'moe_b_router': nrm(ks[14], (N_EXPERTS,), 0.01),
        'moe_w_gate': nrm(ks[15], (DEPTH, N_EXPERTS, D, D_FF_EXPERT), D ** -0.5),
        'moe_w_up': nrm(ks[16], (DEPTH, N_EXPERTS, D, D_FF_EXPERT), D ** -0.5),
        'moe_w_down': nrm(ks[17], (DEPTH, N_EXPERTS, D_FF_EXPERT, D), DN_BETA * D_FF_EXPERT ** -0.5),
        'ln_g': 1.0 + nrm(ks[18], (DEPTH, 2, D), 0.02),
        'ln_b': nrm(ks[19], (DEPTH, 2, D), 0.02),
    }

def second_block(x, gla_w_in, gla_w_gate_up, gla_b_gate, gla_norm_g, gla_w_out,
              nsa_w_in, nsa_w_cmp_k1, nsa_w_cmp_k2, nsa_w_cmp_v1, nsa_w_cmp_v2, nsa_cmp_pe, nsa_w_out,
              moe_w_router, moe_b_router, moe_w_gate, moe_w_up, moe_w_down, ln_g, ln_b):
    for i in range(DEPTH):
        j = i // 2
        if i % 2 == 0:
            h = gla_mixer(x, gla_w_in[j], gla_w_gate_up[j], gla_b_gate[j], gla_norm_g[j], gla_w_out[j])
        else:
            h = nsa_mixer(x, nsa_w_in[j], nsa_w_cmp_k1[j], nsa_w_cmp_k2[j], nsa_w_cmp_v1[j],
                          nsa_w_cmp_v2[j], nsa_cmp_pe[j], nsa_w_out[j])
        x = layer_norm(DN_ALPHA * x + h, ln_g[i, 0], ln_b[i, 0])
        f = moe_ffn(x, moe_w_router, moe_b_router, moe_w_gate[i], moe_w_up[i], moe_w_down[i])
        x = layer_norm(DN_ALPHA * x + f, ln_g[i, 1], ln_b[i, 1])
    return x


def setup_inputs(seed=0):
    out = dict(first_inputs(seed))
    for name, value in second_inputs(seed + 1).items():
        if name != "x":
            out[name + "_2"] = value
    return out


def reference(
    x, p, positions, ffn1_norm, ffn1_w_gu, ffn1_w_down, mix_norm, w_in, conv_w, w_conv_out,
    q_norm, kv_norm, w_uq, w_ukv, w_mla_out, w_o, ffn2_norm, ffn2_w_gu, ffn2_w_down, ple_norm,
    w_ple_gate, w_ple_proj, final_norm, gla_w_in_2, gla_w_gate_up_2, gla_b_gate_2, gla_norm_g_2,
    gla_w_out_2, nsa_w_in_2, nsa_w_cmp_k1_2, nsa_w_cmp_k2_2, nsa_w_cmp_v1_2, nsa_w_cmp_v2_2,
    nsa_cmp_pe_2, nsa_w_out_2, moe_w_router_2, moe_b_router_2, moe_w_gate_2, moe_w_up_2,
    moe_w_down_2, ln_g_2, ln_b_2,
):
    x = first_block(
        x, p, positions, ffn1_norm, ffn1_w_gu, ffn1_w_down, mix_norm, w_in, conv_w, w_conv_out,
        q_norm, kv_norm, w_uq, w_ukv, w_mla_out, w_o, ffn2_norm, ffn2_w_gu, ffn2_w_down,
        ple_norm, w_ple_gate, w_ple_proj, final_norm,
    )
    return second_block(
        x, gla_w_in_2, gla_w_gate_up_2, gla_b_gate_2, gla_norm_g_2, gla_w_out_2, nsa_w_in_2,
        nsa_w_cmp_k1_2, nsa_w_cmp_k2_2, nsa_w_cmp_v1_2, nsa_w_cmp_v2_2, nsa_cmp_pe_2,
        nsa_w_out_2, moe_w_router_2, moe_b_router_2, moe_w_gate_2, moe_w_up_2, moe_w_down_2,
        ln_g_2, ln_b_2,
    )


_drawn_inputs = setup_inputs


def setup_inputs(seed=0):
    import zlib

    import numpy as np

    out = dict(_drawn_inputs(seed))
    spreads = {}
    factors = {'nsa_cmp_pe_2': 2.721}
    for name, (base, spread) in spreads.items():
        noise = np.random.default_rng([zlib.crc32(name.encode()), seed]).standard_normal(out[name].shape)
        drawn = base * np.exp(spread * noise) if base else spread * noise
        out[name] = __import__('jax').numpy.asarray(drawn.astype(out[name].dtype))
    for name, factor in factors.items():
        out[name] = (out[name] * factor).astype(out[name].dtype)
    return out
```

```python
import math
from contextlib import ExitStack, contextmanager

import numpy as np

import concourse.bass as bass
from concourse import mybir

F32 = mybir.dt.float32
F32R = mybir.dt.float32r
BF16 = mybir.dt.bfloat16
I32 = mybir.dt.int32
ALU = mybir.AluOpType
ACT = mybir.ActivationFunctionType
AX = mybir.AxisListType

P = 128
T = 256
TT = T // P
D = 1024
KD = D // P
DEPTH = 2
DFF = 2816
CONV = 512
QL, KVL, ROPE, NOPE, VD, NH = 384, 256, 64, 128, 128, 8
QKD = NOPE + ROPE
SCALE = QKD ** -0.5
CHUNK = 64
EPS, LN_EPS = 1e-6, 1e-5
GH, GDK, GDV, GRANK, GTAU = 4, 128, 256, 16, 16.0
NHEADS, NG, HPG, DH = 16, 4, 4, 64
NCMP = 15
CSTR = 16
NE, EG = 16, 4
ALPHA = (2 * DEPTH) ** 0.25
NEG = -1e30
UNIT = 2048
SLOTS = 3
SIDE = 256
FF_TRIPS = DFF // SIDE
PI = math.pi
TURN_PARTS = (6.25, 0.03125, 0.0019350051879882812, 2 * PI - 6.25 - 0.03125 - 0.0019350051879882812)
HALVES = [(0, 4), (4, 8)]
WHOLE = [(0, 8)]

CONSTS = dict(ident=128, ones=128, mask1=384, causal=384, same_chunk=128, rot=128, cosk=256, sink=256,
              cosc=60, sinc=60, cmask=64, any_key=2, inv_freq=1, lower=16)
LAYER_SMALL = dict(ffn1=8, mix=8, qn=3, kvn=2, conv=12, ffn2=8, ple=8)
LAYER_COLS = sum(LAYER_SMALL.values())
SMALL = dict(layers=DEPTH * LAYER_COLS, final=8, b_gate=4, gla_g=2, ln_g=32, ln_b=32, w_low=128, w_up=512,
             w_router=128, b_router=16, w_gates=384, w2k=256, w2v=128, pe=32)


def offsets(widths):
    at, out = 0, {}
    for name, n in widths.items():
        out[name] = (at, n)
        at += n
    return out, at


CONST_AT, CONST_COLS = offsets(CONSTS)
SMALL_AT, SMALL_COLS = offsets(SMALL)
LAYER_AT, _ = offsets(LAYER_SMALL)


def constants():
    c = np.zeros((P, CONST_COLS), np.float32)

    def put(name, a):
        o, n = CONST_AT[name]
        c[:, o:o + n] = np.asarray(a, np.float32).reshape(a.shape[0], n)

    p = np.arange(P)
    put("ident", np.eye(P))
    put("ones", np.ones((P, P)))
    q = np.concatenate([np.broadcast_to(p[:, None], (P, P)), np.broadcast_to(P + p[:, None], (P, T))], 1)
    k = np.concatenate([np.broadcast_to(p[None], (P, P)), np.broadcast_to(np.arange(T)[None], (P, T))], 1)
    put("mask1", np.where(k // CHUNK <= q // CHUNK, 0.0, NEG))
    put("causal", np.where(k <= q, 0.0, NEG))
    put("same_chunk", (p[:, None] // CHUNK == p[None] // CHUNK) & (p[:, None] <= p[None]))
    rot = np.zeros((P, P))
    for h in range(0, P, DH):
        for i in range(8):
            rot[h + 8 + i, h + i] = -1.0
            rot[h + i, h + 8 + i] = 1.0
    put("rot", rot)
    inv = np.power(np.float32(500000.0), -np.arange(8, dtype=np.float32) * np.float32(2.0 / 16)).astype(np.float32)

    def tables(pos):
        ang = (pos.astype(np.float32)[:, None] * inv[None]).astype(np.float32)
        cos, sin = np.ones((DH, len(pos))), np.zeros((DH, len(pos)))
        cos[:8] = cos[8:16] = np.cos(ang).T
        sin[:8] = sin[8:16] = np.sin(ang).T
        return np.tile(cos, (2, 1)), np.tile(sin, (2, 1))

    ct, st = tables(np.arange(T))
    put("cosk", ct)
    put("sink", st)
    cmp_end = np.arange(NCMP) * CSTR + 2 * CSTR - 1
    ct, st = tables(cmp_end)
    put("cosc", np.repeat(ct, NG, axis=1))
    put("sinc", np.repeat(st, NG, axis=1))
    end = np.concatenate([cmp_end, np.full(32 - NCMP, 10 * T)])
    pos = np.stack([p, P + p], 1)
    seen = end[None, None, :] <= pos[:, :, None]
    put("cmask", np.where(seen, 0.0, NEG))
    put("any_key", seen.any(-1))
    f = np.float32(10000.0) ** (-np.arange(0, ROPE, 2, dtype=np.float32) / np.float32(ROPE))
    put("inv_freq", np.tile(f.astype(np.float32), 4)[:, None])
    lower = np.arange(EG)[None, :] < np.arange(EG)[:, None]
    put("lower", np.broadcast_to(lower[None], (P, EG, EG)))
    return c


def rows(w):
    return w.reshape(w.shape[0] // P, P, w.shape[1]).transpose(1, 0, 2)


def unit(w):
    w = rows(w)
    u = np.zeros((P, UNIT), np.float32)
    u[:, :w.shape[1] * w.shape[2]] = w.reshape(P, -1)
    return u


def halves(w):
    return [unit(w[:, c:c + SIDE]) for c in range(0, w.shape[1], SIDE)]


def feed_forward_units(gate, up, down):
    out = []
    for i in range(gate.shape[1] // SIDE):
        s = slice(i * SIDE, (i + 1) * SIDE)
        out += [unit(gate[:, s]), unit(up[:, s])]
        if i:
            out.append(unit(down[(i - 1) * SIDE:i * SIDE]))
    return out + [unit(down[-SIDE:])]


def weight_stream(a):
    units = []
    for l in range(DEPTH):
        def ffn(n):
            gu = a[f"ffn{n}_w_gu"][l]
            return feed_forward_units(gu[:, :DFF], gu[:, DFF:], a[f"ffn{n}_w_down"][l])

        units += ffn(1)
        w = a["w_in"][l]
        b, c, v, q, kv, kr, gc, gm = np.split(w, np.cumsum([CONV, CONV, CONV, QL, KVL, ROPE, D]), axis=1)
        half = ROPE // 2
        units += [unit(q[:, :SIDE]), unit(q[:, SIDE:]), unit(kv),
                  unit(np.concatenate([np.tile(kr[:, :half], (1, 4)), np.tile(kr[:, half:], (1, 4))], 1))]
        units += halves(c) + halves(v) + halves(b) + halves(gc) + halves(gm)
        uq = a["w_uq"][l].reshape(QL, NH, QKD)
        nope = uq[:, :, :NOPE].reshape(QL, -1)
        r1 = uq[:, :, NOPE:NOPE + half].reshape(QL, -1)
        r2 = uq[:, :, NOPE + half:].reshape(QL, -1)
        units += [unit(nope[:, :512]), unit(nope[:, 512:]), unit(np.concatenate([r1, r2], 1))]
        ukv = a["w_ukv"][l].reshape(KVL, NH, NOPE + VD)
        units += [unit(ukv[:, :, :NOPE].reshape(KVL, -1)), unit(ukv[:, :, NOPE:].reshape(KVL, -1))]
        units += [unit(a["w_conv_out"][l][:, :512]), unit(a["w_conv_out"][l][:, 512:])]
        units += halves(a["w_mla_out"][l]) + halves(a["w_o"][l])
        units += ffn(2)
        units += halves(a["w_ple_gate"][l])
        units += [unit(a["w_ple_proj"][l][:, :512]), unit(a["w_ple_proj"][l][:, 512:])]

    def moe(l):
        out = []
        for e in range(NE):
            out += [unit(a["moe_w_gate_2"][l, e]), unit(a["moe_w_up_2"][l, e])]
            if e:
                out.append(unit(a["moe_w_down_2"][l, e - 1]))
        return out + [unit(a["moe_w_down_2"][l, NE - 1])]

    w = a["gla_w_in_2"][0]
    nk, nv = GH * GDK, GH * GDV
    q, k, v, _, r = np.split(w, np.cumsum([nk, nk, nv, GRANK]), axis=1)
    units += halves(q) + halves(k) + [unit(v[i * SIDE:(i + 1) * SIDE]) for i in range(4)] + halves(r)
    units += halves(a["gla_w_out_2"][0]) + moe(0)
    w = a["nsa_w_in_2"][0]
    n = NG * DH
    q, kc, vc, ks, vs, kw, vw, _ = np.split(w, np.cumsum([NHEADS * DH] + [n] * 6), axis=1)

    def twice(m):
        m = m.reshape(D, NG, 1, DH)
        return np.concatenate([m, m], 2).reshape(D, NG * 2 * DH)

    units += halves(q) + halves(twice(kc)) + halves(twice(vc)) + halves(twice(ks)) + halves(twice(kw))
    vv = np.concatenate([vs, vw], 1)
    units += [unit(vv[:512]), unit(vv[512:])]
    for name in ("nsa_w_cmp_k1_2", "nsa_w_cmp_v1_2"):
        w1 = a[name][0]
        units += [unit(w1[:, :P]), unit(w1[:, P:])]
    units += halves(a["nsa_w_out_2"][0]) + moe(1)
    units += [np.zeros((P, UNIT), np.float32)] * (-len(units) % SLOTS or SLOTS)
    return np.stack(units)


def small_operands(a):
    s = np.zeros((P, SMALL_COLS), np.float32)

    def put(name, v):
        o, n = SMALL_AT[name]
        s[:v.shape[0], o:o + n] = v.reshape(v.shape[0], n)

    def col(v):
        return v.reshape(-1, P).T

    layers = []
    for l in range(DEPTH):
        conv = a["conv_w"][l].reshape(3, CONV // P, P).transpose(2, 1, 0).reshape(P, -1)
        layers += [col(a["ffn1_norm"][l]), col(a["mix_norm"][l]), col(a["q_norm"][l]), col(a["kv_norm"][l]), conv,
                   col(a["ffn2_norm"][l]), col(a["ple_norm"][l])]
    put("layers", np.concatenate(layers, 1))
    put("final", col(a["final_norm"]))
    put("b_gate", col(a["gla_b_gate_2"][0]))
    put("gla_g", col(a["gla_norm_g_2"][0]))
    put("ln_g", col(a["ln_g_2"].reshape(-1)))
    put("ln_b", col(a["ln_b_2"].reshape(-1)))
    lo = 2 * GH * GDK + GH * GDV
    put("w_low", rows(a["gla_w_in_2"][0][:, lo:lo + GRANK]))
    put("w_up", a["gla_w_gate_up_2"][0])
    put("w_router", rows(a["moe_w_router_2"]))
    put("b_router", np.broadcast_to(a["moe_b_router_2"][None], (P, NE)))
    put("w_gates", rows(a["nsa_w_in_2"][0][:, -3 * NHEADS:]))
    w2k = rows(a["nsa_w_cmp_k2_2"][0])
    put("w2k", np.concatenate([w2k, w2k], 2))
    put("w2v", rows(a["nsa_w_cmp_v2_2"][0]))
    pe = a["nsa_cmp_pe_2"][0].reshape(16, P).T
    put("pe", np.stack([pe, pe], 2))
    return s


class Seen:

    def __init__(self, who, per_trip):
        self.who, self.per_trip, self.count, self.loops = who, per_trip, {}, []

    def more(self, sem, n=1, tag=""):
        key = sem.name + tag
        self.count[key] = self.count.get(key, 0) + n
        return self.at(sem, tag)

    def at(self, sem, tag=""):
        key = sem.name + tag
        value = self.count.get(key, 0)
        for label, trip in self.loops:
            step = self.per_trip.get((self.who, label, key), 0)
            if step:
                value = trip * step + value
        return value

    @contextmanager
    def loop(self, engine, label, trips):
        before = dict(self.count)
        with engine.Fori(0, trips) as trip:
            self.loops.append((label, trip))
            yield trip
            self.loops.pop()
        for key, n in self.count.items():
            step = n - before.get(key, 0)
            self.per_trip[(self.who, label, key)] = step
            self.count[key] = n + step * (trips - 1)


def two_blocks(nc, per_trip, stream, consts, smalls, x_in, p_in, pos_in, out):
    n_units = stream.shape[0]
    with ExitStack() as ctx:
        def sb(name, shape, dt=F32):
            return ctx.enter_context(nc.sbuf_tensor(name, shape, dt))

        def sem(name):
            return ctx.enter_context(nc.semaphore(name))

        raw = sb("raw", [P, SLOTS, UNIT])
        w_hi = sb("w_hi", [P, SLOTS, UNIT], F32R)
        w_lo = sb("w_lo", [P, SLOTS, UNIT], F32R)
        h = sb("h", [P, KD, T])
        x32 = sb("x32", [P, KD, T])
        x_hi = sb("x_hi", [P, KD, T], F32R)
        x_lo = sb("x_lo", [P, KD, T], F32R)
        y_hi = sb("y_hi", [P, KD, T], F32R)
        y_lo = sb("y_lo", [P, KD, T], F32R)
        rstd = sb("rstd", [P, T])
        side = sb("side", [P, 2, T])
        act_gate = sb("act_gate", [P, 2, T])
        cst = sb("cst", [P, CONST_COLS])
        sml = sb("sml", [P, SMALL_COLS])
        cur = sb("cur", [P, LAYER_COLS])
        pe_hi = sb("pe_hi", [P, 32], F32R)
        pe_lo = sb("pe_lo", [P, 32], F32R)
        zero = sb("zero", [P, 512], BF16)
        stats = sb("stats", [P, 64])
        arena = sb("arena", [P, 16 * 1024])

        def view(at, *shape):
            n = math.prod(shape)
            v = arena[:, at:at + n]
            if len(shape) == 1:
                return v
            names = "abcd"[:len(shape)]
            return v.rearrange(f"p ({' '.join(names)}) -> p {' '.join(names)}",
                               **{c: s for c, s in zip(names, shape)})

        def const(name):
            o, n = CONST_AT[name]
            return cst[:, o:o + n]

        def small(name):
            o, n = SMALL_AT[name]
            return sml[:, o:o + n]

        def gain(name):
            o, n = LAYER_AT[name]
            return cur[:, o:o + n]

        ident, ones = const("ident"), const("ones")

        conv_c = view(0, 4, T)
        conv_z = view(1024, 4, T + 2)
        keys_n = view(0, NH, T)
        q_c = view(2060, 3, T)
        kv_c = view(2060 + 768, 2, T)
        k_r = view(2060 + 1280, 2, T)
        vals = view(2060, TT, NH * VD)
        g_conv = view(4108, KD, T)
        g_mla = view(6156, KD, T)
        q_n = view(8204, NH, T)
        q_rot = view(10252, 4, T)
        k_rot = view(11276, 8, T)
        cos1 = view(13324, T)
        sin1 = view(13580, T)
        p_all = view(13836, DEPTH * 2, T)
        probs1 = view(14860, 2, 384)
        probs_t1 = view(15628, 384)
        merged = x32
        rope_a, rope_b = side, act_gate

        gla_q = view(0, GH, T)
        gla_k = view(1024, GH, T)
        gla_z = view(2048, GH, T)
        gla_t = view(3072, GH, T)
        gla_b = view(4096, GH, T)
        gla_carry = view(5120, GH, T)
        gla_scores = view(5120, GH * TT, P)
        gla_eb = view(6144, GH, T)
        gla_kend = view(7168, GH, T)
        gla_v = view(8192, TT, GH * GDV)
        gla_r = view(10240, KD, T)
        gla_kt = view(12288, TT, GH, 2, P)
        gla_state = view(2048, GH, 3, GDV)
        gla_rs = view(14336, GH, T)
        gla_low = view(15360, T)
        sq8 = view(12288, KD, T)

        gate_rows = view(0, NE, T)
        gate_pad = view(4096, TT, P)
        gate_t = view(4352, T)
        r_s, r_b, r_sel, r_tmp = (view(4608 + 32 * i, TT * NE) for i in range(4))
        r_gt, r_ge = view(4736, 128), view(4864, 128)
        r_rank, r_grp, r_win, r_den = view(4992, 32), view(5024, 8), view(5032, 8), view(5040, 2)

        nsa_q = view(0, KD, T)
        nsa_ks = view(2048, NG, 2, T)
        nsa_kw = view(4096, NG, 2, T)
        nsa_v = view(6144, 2, TT, NG, 192)
        nsa_k32 = view(9216, 2, NG, T)
        nsa_c32 = view(11264, 2, NG, T)
        nsa_hidr = view(13312, 2, NG, P)
        nsa_vc = view(14336, NG, 2, P)
        nsa_s = view(9216, TT, NHEADS, 32)
        nsa_p = view(10240, TT, NHEADS, 32)
        nsa_pt = view(11264, NG, T)
        nsa_probs = view(12288, 2, 384)
        nsa_probs_t = view(13312, 384)
        nsa_hid = view(15360, 4, 60)
        nsa_kcm = view(15600, 64)
        nsa_kct = view(15664, 64)
        nsa_kc = view(15728, NG, 2, 32)
        nsa_gates = view(15984, TT, 48)
        nsa_st = view(16080, 4, 32)

        psa = ctx.enter_context(nc.psum_tensor("psa", [P, 4, 512], F32))
        psd = ctx.enter_context(nc.psum_tensor("psd", [P, 4, 512], F32))

        inputs_in = sem("inputs_in")
        raw_full = [sem(f"raw_full{s}") for s in range(SLOTS)]
        hi_done = sem("hi_done")
        lo_done = sem("lo_done")
        unit_done = sem("unit_done")
        evac = sem("evac")
        gate_out = sem("gate_out")
        side_ready = sem("side_ready")
        silu_done = sem("silu_done")
        hid_hi = sem("hid_hi")
        hid_ready = sem("hid_ready")
        norm_in = sem("norm_in")
        sq_ready = sem("sq_ready")
        stat_done = sem("stat_done")
        mean_done = sem("mean_done")
        xm_ready = sem("xm_ready")
        rstd_ready = sem("rstd_ready")
        x32_ready = sem("x32_ready")
        xh_ready = sem("xh_ready")
        x_ready = sem("x_ready")
        s_done = sem("s_done")
        nmax_ready = sem("nmax_ready")
        exp_done = sem("exp_done")
        p_ready = sem("p_ready")
        t_done = sem("t_done")
        pt_ready = sem("pt_ready")
        pv_done = sem("pv_done")
        o_done = sem("o_done")
        for_act = sem("for_act")
        for_pe = sem("for_pe")
        act_out = sem("act_out")
        pe_out = sem("pe_out")
        pe_to_act = sem("pe_to_act")
        dve_step = sem("dve_step")
        act_step = sem("act_step")
        result_ready = sem("result_ready")
        stored = sem("stored")

        block = ctx.enter_context(nc.Block())

        def pair(bank):
            return psa[:, bank, :].rearrange("p (a t) -> p a t", a=2)

        @block.sync
        def _(sp):
            seen = Seen("sp", per_trip)
            for dst, src in ((cst[:], consts), (sml[:], smalls), (h[:], x_in), (p_all, p_in),
                             (x32[:, 0, :].bitcast(I32), pos_in)):
                sp.dma_start(dst, src).then_inc(inputs_in, 16)
            with seen.loop(sp, "units", n_units // SLOTS) as i:
                for s in range(SLOTS):
                    sp.wait_ge(lo_done, seen.more(lo_done))
                    sp.dma_start(raw[:, s, :], stream[i * SLOTS + s]).then_inc(raw_full[s], 16)
            sp.wait_ge(result_ready, 1)
            sp.dma_start(out, h[:]).then_inc(stored, 16)
            sp.wait_ge(stored, 16)

        @block.scalar
        def _(act):
            seen = Seen("act", per_trip)
            seen.more(unit_done, SLOTS, "result")
            ring = [0]

            def step(ins):
                ins.then_inc(act_step, 1)
                act.wait_ge(act_step, seen.more(act_step))

            def split_hi():
                s = ring[0] % SLOTS
                ring[0] += 1
                act.wait_ge(raw_full[s], seen.more(raw_full[s], 16))
                act.wait_ge(unit_done, seen.more(unit_done, tag="slot"))
                act.activation(w_hi[:, s, :], raw[:, s, :], ACT.Copy).then_inc(hi_done, 1)

            def split_x(pieces, src, hi, to=0):
                for a, b in pieces:
                    act.wait_ge(x32_ready, seen.more(x32_ready))
                    act.activation(hi[:, to + a:to + b, :], src[:, a:b, :], ACT.Copy).then_inc(xh_ready, 1)

            def rms(src, n, features, eps, sq):
                act.activation(sq[:, 0:n, :], src[:, 0:n, :], ACT.Square).then_inc(sq_ready, 1)
                act.wait_ge(stat_done, seen.more(stat_done))
                step(act.activation(rstd[:], psa[:, 3, 0:T], ACT.Ln, bias=eps, scale=1.0 / features))
                act.activation(rstd[:], rstd[:], ACT.Exp, scale=-0.5).then_inc(rstd_ready, 1)

            def norm(src, n, features):
                act.wait_ge(norm_in, seen.more(norm_in))
                rms(src, n, features, EPS, x32)

            def layer_norm(split=True):
                act.wait_ge(xm_ready, seen.more(xm_ready))
                rms(x32, KD, D, LN_EPS, sq8)
                if split:
                    split_x(HALVES, h, x_hi)

            def units(n, after=None):
                for j in range(n):
                    split_hi()
                    done = seen.more(unit_done, tag="result")
                    if after is not None:
                        act.wait_ge(unit_done, done)
                        after(j)

            def feed_forward(label, trips, last=False):
                def trip(first):
                    split_hi()
                    act.wait_ge(unit_done, seen.more(unit_done, tag="result"))
                    act.activation(act_gate[:], pair(0), ACT.Silu).then_inc(silu_done, 1)
                    split_hi()
                    seen.more(unit_done, tag="result")
                    if not first:
                        split_hi()
                        act.wait_ge(unit_done, seen.more(unit_done, tag="result"))
                    act.wait_ge(side_ready, seen.more(side_ready))
                    act.activation(y_hi[:, 0:2, :], side[:], ACT.Copy).then_inc(hid_hi, 1)

                trip(True)
                with seen.loop(act, label, trips - 1):
                    trip(False)
                if not last:
                    split_hi()
                seen.more(unit_done, tag="result")

            def activate_to(dst, func):
                def after(j):
                    act.activation(dst[:, 2 * j:2 * j + 2, :], pair(j % 4), func).then_inc(gate_out, 1)
                return after

            def softmax_item(t, scale, probs):
                act.wait_ge(nmax_ready, seen.more(nmax_ready))
                s = t % 2
                b = 8 * s
                act.activation(probs[:, s, 0:P], probs[:, s, 0:P], ACT.Exp, bias=stats[:, b + 2:b + 3],
                               scale=scale, accum_out=stats[:, b + 4:b + 5])
                act.activation(probs[:, s, P:384], probs[:, s, P:384], ACT.Exp, bias=stats[:, b + 3:b + 4],
                               scale=scale, accum_out=stats[:, b + 5:b + 6]).then_inc(exp_done, 1)

            act.wait_ge(for_act, seen.more(for_act))
            act.activation(sin1, x32[:, 3, :], ACT.Sin)
            act.activation(cos1, x32[:, 4, :], ACT.Sin)
            act.activation(pe_hi[:], small("pe"), ACT.Copy).then_inc(act_out, 1)
            split_hi()
            split_hi()
            with seen.loop(act, "layers", DEPTH) as l:
                norm(h, KD, D)
                split_x(HALVES, x32, x_hi)
                feed_forward("ffn1", FF_TRIPS)
                norm(h, KD, D)
                split_x(HALVES, x32, x_hi)
                units(4 + 6)
                split_x([(0, 4)], conv_c, y_hi)
                units(4, activate_to(g_conv, ACT.Sigmoid))
                units(4, activate_to(g_mla, ACT.Sigmoid))
                norm(q_c, 3, QL)
                split_x([(0, 3)], x32, x_hi)
                norm(kv_c, 2, KVL)
                split_x([(0, 2)], x32, x_hi, to=3)
                units(3 + 1 + 1 + 2)
                for t in range(NH):
                    softmax_item(t, SCALE, probs1)
                split_x(WHOLE, q_n, y_hi)
                units(4)
                split_x(WHOLE, merged, x_hi)
                units(4)
                norm(h, KD, D)
                split_x(HALVES, x32, x_hi)
                feed_forward("ffn2", FF_TRIPS)
                act.wait_ge(norm_in, seen.more(norm_in))
                act.activation(y_hi[:, 0:2, :], p_all[:, bass.ds(l * 2, 2), :], ACT.Copy).then_inc(act_out, 1)
                rms(h, KD, D, EPS, x32)
                split_x(HALVES, x32, x_hi)
                units(4, activate_to(g_conv, ACT.Sigmoid))
                units(2)
            norm(h, KD, D)
            split_x(HALVES, h, x_hi)

            units(2 + 2 + 4)
            units(4, activate_to(gla_r, ACT.Silu))
            act.wait_ge(for_act, seen.more(for_act))
            step(act.activation(gla_t, gla_z, ACT.Abs))
            step(act.activation(gla_t, gla_t, ACT.Exp, scale=-1.0))
            act.activation(gla_t, gla_t, ACT.Ln, bias=1.0).then_inc(act_out, 1)
            act.wait_ge(for_act, seen.more(for_act))
            act.activation(gla_eb, gla_b, ACT.Exp, scale=1.0 / GTAU)
            act.activation(gla_z, gla_b, ACT.Exp, scale=-1.0 / GTAU)
            act.activation(gla_kend, gla_t, ACT.Exp, scale=1.0 / GTAU).then_inc(act_out, 1)
            act.wait_ge(for_act, seen.more(for_act))
            act.activation(sq8, x32[:], ACT.Square).then_inc(sq_ready, 1)
            act.wait_ge(stat_done, seen.more(stat_done))
            step(act.activation(gla_rs, psd[:, 0:2, :].rearrange("p a (b t) -> p (a b) t", b=2), ACT.Ln,
                                bias=LN_EPS, scale=1.0 / GDV))
            act.activation(gla_rs, gla_rs, ACT.Exp, scale=-0.5).then_inc(rstd_ready, 1)
            split_x(WHOLE, x32, y_hi)
            units(4)
            layer_norm()

            def moe(label, last=False):
                act.wait_ge(pe_to_act, seen.more(pe_to_act))
                act.activation(r_s, psd[:, 0, 0:TT * NE], ACT.Sigmoid).then_inc(act_out, 1)
                feed_forward(label, NE, last)

            moe("moe0")
            layer_norm()

            units(4 + 2 + 2)
            act.wait_ge(x32_ready, seen.more(x32_ready))
            for a in range(2):
                act.activation(y_hi[:, 4 * a:4 * a + 4, 0:T - 1], nsa_c32[:, a, :, 0:T - 1],
                               ACT.Copy).then_inc(xh_ready, 1)
            units(2 + 2 + 2)
            act.wait_ge(pe_to_act, seen.more(pe_to_act))
            act.activation(nsa_gates, psd[:, 0, 0:96].rearrange("p (a c) -> p a c", a=2),
                           ACT.Sigmoid).then_inc(act_out, 1)
            for j in range(4):
                split_hi()
                seen.more(unit_done, tag="result")
                act.wait_ge(for_act, seen.more(for_act))
                act.activation(nsa_hid[:, j, :], nsa_hid[:, j, :], ACT.Silu).then_inc(act_out, 1)
            act.wait_ge(for_act, seen.more(for_act))
            act.activation(nsa_p, nsa_s, ACT.Exp, scale=DH ** -0.5).then_inc(act_out, 1)
            for t in range(2 * NHEADS):
                softmax_item(t, DH ** -0.5, nsa_probs)
            split_x(WHOLE, nsa_q, y_hi)
            units(4)
            layer_norm()
            moe("moe1", last=True)
            layer_norm(split=False)

        @block.vector
        def _(dve):
            seen = Seen("dve", per_trip)
            seen.more(unit_done, SLOTS, "result")
            ring = [0]

            def step(ins):
                ins.then_inc(dve_step, 1)
                dve.wait_ge(dve_step, seen.more(dve_step))

            def mark(signal):
                dve.drain().then_inc(signal, 1)

            def settle():
                dve.drain()

            def split_lo():
                s = ring[0] % SLOTS
                ring[0] += 1
                dve.wait_ge(hi_done, seen.more(hi_done))
                dve.tensor_tensor(w_lo[:, s, :], raw[:, s, :], w_hi[:, s, :], ALU.subtract).then_inc(lo_done, 1)

            def split_x(pieces, src, hi, lo, to=0):
                for a, b in pieces:
                    dve.wait_ge(xh_ready, seen.more(xh_ready))
                    dve.tensor_tensor(lo[:, to + a:to + b, :], src[:, a:b, :], hi[:, to + a:to + b, :],
                                      ALU.subtract).then_inc(x_ready, 1)

            def norm(src, gains, pieces, dst=x32):
                dve.wait_ge(rstd_ready, seen.more(rstd_ready))
                for a, b in pieces:
                    for k in range(a, b):
                        ins = dve.scalar_tensor_tensor(dst[:, k, :], src[:, k, :], gains[:, k:k + 1], rstd[:],
                                                       ALU.mult, ALU.mult)
                    ins.then_inc(x32_ready, 1)

            def layer_norm(i, split=True):
                dve.wait_ge(mean_done, seen.more(mean_done))
                mean = psd[:, 0, 0:T].unsqueeze(1).broadcast_to([P, KD, T])
                dve.scalar_tensor_tensor(x32[:], mean, -1.0 / D, h[:], ALU.mult, ALU.add).then_inc(xm_ready, 1)
                dve.wait_ge(rstd_ready, seen.more(rstd_ready))
                step(dve.tensor_tensor(x32[:], x32[:], rstd[:].unsqueeze(1).broadcast_to([P, KD, T]), ALU.mult))
                g, b = small("ln_g"), small("ln_b")
                for lo, hi in HALVES:
                    for k in range(lo, hi):
                        c = i * KD + k
                        ins = dve.tensor_scalar(h[:, k, :], x32[:, k, :], g[:, c:c + 1], b[:, c:c + 1],
                                                ALU.mult, ALU.add)
                    if split:
                        ins.then_inc(x32_ready, 1)
                if split:
                    split_x(HALVES, h, x_hi, x_lo)
                else:
                    ins.then_inc(result_ready, 1)

            def units(n, after, signal=evac, last=None):
                for j in range(n):
                    split_lo()
                    done = seen.more(unit_done, tag="result")
                    if after is not None:
                        settle()
                        dve.wait_ge(unit_done, done)
                        ins = after(j)
                        if ins is not None:
                            ins.then_inc(last if last is not None and j == n - 1 else signal, 1)

            def feed_forward(label, trips, gates=None, alpha=None, last=False):
                def trip(i, first):
                    split_lo()
                    seen.more(unit_done, tag="result")
                    split_lo()
                    settle()
                    dve.wait_ge(unit_done, seen.more(unit_done, tag="result"))
                    dve.wait_ge(silu_done, seen.more(silu_done))
                    if gates is None:
                        dve.tensor_tensor(side[:], pair(1), act_gate[:], ALU.mult).then_inc(side_ready, 1)
                    else:
                        gate = gates[:, bass.ds(i, 1), :] if not isinstance(i, int) else gates[:, i:i + 1, :]
                        step(dve.tensor_tensor(side[:], pair(1), gate.broadcast_to([P, 2, T]), ALU.mult))
                        dve.tensor_tensor(side[:], side[:], act_gate[:], ALU.mult).then_inc(side_ready, 1)
                    if not first:
                        split_lo()
                        seen.more(unit_done, tag="result")
                    dve.wait_ge(hid_hi, seen.more(hid_hi))
                    dve.tensor_tensor(y_lo[:, 0:2, :], side[:], y_hi[:, 0:2, :],
                                      ALU.subtract).then_inc(hid_ready, 1)

                trip(0, True)
                with seen.loop(dve, label, trips - 1) as i:
                    trip(i + 1, False)
                if not last:
                    split_lo()
                dve.wait_ge(unit_done, seen.more(unit_done, tag="result"))
                for b in range(4):
                    hb = h[:, 2 * b:2 * b + 2, :]
                    db = psd[:, b, :].rearrange("p (a t) -> p a t", a=2)
                    if alpha is None:
                        ins = dve.scalar_tensor_tensor(hb, db, 0.5, hb, ALU.mult, ALU.add)
                    else:
                        ins = dve.scalar_tensor_tensor(hb, hb, alpha, db, ALU.mult, ALU.add)
                ins.then_inc(norm_in, 1)

            def copy_to(dst, width=2):
                return lambda j: dve.tensor_copy(dst[:, 2 * j:2 * j + width, :], pair(j % 4)[:, 0:width, :])

            def four(half):
                return psa[:, 2 * half:2 * half + 2, :].rearrange("p a (b t) -> p (a b) t", b=2)

            def attention(items, scale, mask, probs, probs_t, write_out, gate=None, per_out=1):
                def maximum(t):
                    s, b = t % 2, 8 * (t % 2)
                    dve.wait_ge(s_done, seen.more(s_done))
                    step(dve.tensor_tensor(probs[:, s, :], psd[:, s, 0:384], mask, ALU.add))
                    dve.tensor_reduce(stats[:, b:b + 1], probs[:, s, 0:P], AX.X, ALU.max)
                    step(dve.tensor_reduce(stats[:, b + 1:b + 2], probs[:, s, P:384], AX.X, ALU.max))
                    dve.tensor_scalar(stats[:, b + 2:b + 4], stats[:, b:b + 2], -scale, None,
                                      ALU.mult).then_inc(nmax_ready, 1)

                def normalize(t):
                    s, b = t % 2, 8 * (t % 2)
                    dve.wait_ge(exp_done, seen.more(exp_done))
                    step(dve.reciprocal(stats[:, b + 6:b + 8], stats[:, b + 4:b + 6]))
                    if gate is not None:
                        step(dve.tensor_tensor(stats[:, b + 6:b + 8], stats[:, b + 6:b + 8], gate(t), ALU.mult))
                    dve.tensor_scalar(probs[:, s, 0:P], probs[:, s, 0:P], stats[:, b + 6:b + 7], None, ALU.mult)
                    dve.tensor_scalar(probs[:, s, P:384], probs[:, s, P:384], stats[:, b + 7:b + 8], None,
                                      ALU.mult).then_inc(p_ready, 1)

                def copy_transposed(t):
                    dve.wait_ge(t_done, seen.more(t_done))
                    if t > 0:
                        dve.wait_ge(pv_done, seen.more(pv_done))
                    dve.tensor_copy(probs_t, psd[:, 2, 0:384]).then_inc(pt_ready, 1)

                for t in range(items + 3):
                    if 0 <= t - 2 < items:
                        copy_transposed(t - 2)
                    if t < items:
                        maximum(t)
                    if 0 <= t - 1 < items:
                        normalize(t - 1)
                    if 0 <= t - 3 and (t - 3) % per_out == per_out - 1:
                        if t - 3 == items - 1:
                            dve.wait_ge(pv_done, seen.more(pv_done))
                        write_out((t - 3) // per_out).then_inc(o_done, 1)

            dve.memset(zero[:], 0.0)
            dve.memset(k_rot, 0.0).then_inc(for_pe, 1)
            dve.sem_inc(lo_done, SLOTS)
            dve.sem_inc(unit_done, SLOTS)
            dve.wait_ge(inputs_in, 16 * 5)
            pos = x32[:, 0, :].bitcast(I32)
            step(dve.tensor_copy(x32[:, 1, :], pos))
            step(dve.tensor_scalar(x32[:, 1, :], x32[:, 1, :], const("inv_freq"), None, ALU.mult))
            magic = 1.5 * 2.0 ** 23
            for dst, turn in ((3, 0.0), (4, 0.25)):
                step(dve.tensor_scalar(x32[:, 2, :], x32[:, 1, :], 1.0 / (2.0 * PI), turn, ALU.mult, ALU.add))
                step(dve.tensor_scalar(x32[:, 2, :], x32[:, 2, :], magic, None, ALU.add))
                step(dve.tensor_scalar(x32[:, 2, :], x32[:, 2, :], -magic, None, ALU.add))
                src, rest = 1, 2.0 * PI
                for part in TURN_PARTS:
                    step(dve.scalar_tensor_tensor(x32[:, dst, :], x32[:, 2, :], -part, x32[:, src, :],
                                                  ALU.mult, ALU.add))
                    src = dst
                step(dve.tensor_scalar(x32[:, dst, :], x32[:, dst, :], 2.0 * PI * turn, None, ALU.add))
                step(dve.tensor_scalar(x32[:, dst, :], x32[:, dst, :], 3.1415925, -3.1415925, ALU.min, ALU.max))
            mark(for_act)
            dve.wait_ge(act_out, seen.more(act_out))
            dve.tensor_tensor(pe_lo[:], small("pe"), pe_hi[:], ALU.subtract)
            mark(norm_in)
            split_lo()
            split_lo()

            with seen.loop(dve, "layers", DEPTH) as l:
                settle()
                step(dve.tensor_copy(cur[:], sml[:, bass.ds(l * LAYER_COLS, LAYER_COLS)]))
                norm(h, gain("ffn1"), HALVES)
                split_x(HALVES, x32, x_hi, x_lo)
                feed_forward("ffn1", FF_TRIPS)
                norm(h, gain("mix"), HALVES)
                split_x(HALVES, x32, x_hi, x_lo)
                low_rank = [(q_c[:, 0:2, :], 2), (q_c[:, 2:3, :], 1), (kv_c, 2), (k_r, 2)]
                units(4, lambda j: dve.tensor_copy(low_rank[j][0], pair(j)[:, 0:low_rank[j][1], :]))
                dve.memset(conv_z[:, :, 0:2], 0.0)
                units(2, copy_to(conv_c))

                def times_c(j):
                    return dve.tensor_tensor(conv_z[:, 2 * j:2 * j + 2, 2:T + 2], pair(2 + j),
                                             conv_c[:, 2 * j:2 * j + 2, :], ALU.mult)
                units(2, times_c)
                settle()
                taps = gain("conv")
                for tap in range(3):
                    for k in range(4):
                        w = taps[:, 3 * k + tap:3 * k + tap + 1]
                        z = conv_z[:, k, tap:tap + T]
                        if tap == 0:
                            ins = dve.tensor_scalar(conv_c[:, k, :], z, w, None, ALU.mult)
                        else:
                            ins = dve.scalar_tensor_tensor(conv_c[:, k, :], z, w, conv_c[:, k, :],
                                                           ALU.mult, ALU.add)
                    step(ins)
                units(2, lambda j: dve.tensor_tensor(conv_c[:, 2 * j:2 * j + 2, :], pair(j),
                                                     conv_c[:, 2 * j:2 * j + 2, :], ALU.mult))
                mark(x32_ready)
                split_x([(0, 4)], conv_c, y_hi, y_lo)
                units(8, None)
                mark(norm_in)
                norm(q_c, gain("qn"), [(0, 3)])
                split_x([(0, 3)], x32, x_hi, x_lo)
                mark(norm_in)
                norm(kv_c, gain("kvn"), [(0, 2)])
                split_x([(0, 2)], x32, x_hi, x_lo, to=3)
                dve.wait_ge(gate_out, seen.more(gate_out, 8))
                dve.tensor_tensor(rope_a[:, 0, :], k_r[:, 0, :], cos1, ALU.mult)
                dve.tensor_tensor(rope_a[:, 1, :], k_r[:, 1, :], sin1, ALU.mult)
                dve.tensor_tensor(rope_b[:, 0, :], k_r[:, 1, :], cos1, ALU.mult)
                step(dve.tensor_tensor(rope_b[:, 1, :], k_r[:, 0, :], sin1, ALU.mult))
                for j in range(4):
                    r = slice(32 * j, 32 * j + 32)
                    dve.tensor_tensor(k_rot[r, 2 * j, :], rope_a[r, 0, :], rope_a[r, 1, :], ALU.subtract)
                    ins = dve.tensor_tensor(k_rot[r, 2 * j + 1, :], rope_b[r, 0, :], rope_b[r, 1, :], ALU.add)
                step(ins)

                def query(j):
                    if j < 2:
                        return dve.tensor_copy(q_n[:, 4 * j:4 * j + 4, :], four(j % 2))
                    c = cos1.unsqueeze(1).broadcast_to([P, 2, T])
                    s = sin1.unsqueeze(1).broadcast_to([P, 2, T])
                    dve.tensor_tensor(rope_a[:], pair(0), c, ALU.mult)
                    step(dve.tensor_tensor(rope_b[:], pair(1), s, ALU.mult))
                    step(dve.tensor_tensor(q_rot[:, 0:2, :], rope_a[:], rope_b[:], ALU.subtract))
                    dve.tensor_tensor(rope_a[:], pair(1), c, ALU.mult)
                    step(dve.tensor_tensor(rope_b[:], pair(0), s, ALU.mult))
                    return dve.tensor_tensor(q_rot[:, 2:4, :], rope_a[:], rope_b[:], ALU.add)
                units(3, query)
                units(1, lambda j: dve.tensor_copy(keys_n, psa[:].rearrange("p a (b t) -> p (a b) t", b=2)))
                units(1, lambda j: dve.tensor_copy(vals, psa[:].rearrange("p (a b) t -> p a (b t)", a=2)))
                units(2, lambda j: dve.tensor_tensor(merged[:, 4 * j:4 * j + 4, :], four(j % 2),
                                                     g_conv[:, 4 * j:4 * j + 4, :], ALU.mult))
                attention(NH, SCALE, const("mask1"), probs1, probs_t1,
                          lambda i: dve.tensor_copy(q_n[:, i, :], psd[:, 3, 0:T]))
                mark(x32_ready)
                split_x(WHOLE, q_n, y_hi, y_lo)

                def merge(j):
                    m = merged[:, 2 * j:2 * j + 2, :]
                    step(dve.tensor_tensor(side[:], pair(j), g_mla[:, 2 * j:2 * j + 2, :], ALU.mult))
                    return dve.tensor_tensor(m, m, side[:], ALU.add)
                units(4, merge)
                mark(x32_ready)
                split_x(WHOLE, merged, x_hi, x_lo)

                def residual(j):
                    hj = h[:, 2 * j:2 * j + 2, :]
                    return dve.tensor_tensor(hj, hj, pair(j), ALU.add)
                units(4, residual, last=norm_in)
                norm(h, gain("ffn2"), HALVES)
                split_x(HALVES, x32, x_hi, x_lo)
                feed_forward("ffn2", FF_TRIPS)
                dve.wait_ge(act_out, seen.more(act_out))
                dve.tensor_tensor(y_lo[:, 0:2, :], p_all[:, bass.ds(l * 2, 2), :], y_hi[:, 0:2, :],
                                  ALU.subtract).then_inc(x_ready, 1)
                norm(h, gain("ple"), HALVES)
                split_x(HALVES, x32, x_hi, x_lo)
                units(4, None)
                dve.wait_ge(gate_out, seen.more(gate_out, 4))

                def embed(j):
                    hj, gj = h[:, 4 * j:4 * j + 4, :], g_conv[:, 4 * j:4 * j + 4, :]
                    step(dve.tensor_tensor(gj, four(j), gj, ALU.mult))
                    return dve.tensor_tensor(hj, hj, gj, ALU.add)
                units(2, embed, last=norm_in)

            norm(h, small("final"), HALVES, dst=h)
            split_x(HALVES, h, x_hi, x_lo)

            units(2, copy_to(gla_q))
            units(2, lambda j: dve.tensor_copy(gla_k[:, 2 * j:2 * j + 2, :], pair(2 + j)))
            units(4, lambda j: None if j < 3 else
                  dve.tensor_copy(gla_v, psa[:].rearrange("p (a b) t -> p a (b t)", a=2)))
            units(4, None)
            dve.memset(gla_carry, 1.0)
            settle()
            dve.wait_ge(pe_out, seen.more(pe_out))
            step(dve.memset(gla_carry.rearrange("p h (n c) -> p (h n) c", c=CHUNK)[:, :, 0:1], 0.0))
            dve.tensor_copy(gla_low[0:GRANK, :], psd[0:GRANK, 0, 0:T]).then_inc(for_pe, 1)
            dve.wait_ge(pe_out, seen.more(pe_out))
            for i in range(GH):
                dve.tensor_scalar(gla_z[:, i, :], psd[:, 1 + i // 2, (i % 2) * T:(i % 2) * T + T],
                                  small("b_gate")[:, i:i + 1], None, ALU.add)
            mark(for_act)
            dve.wait_ge(act_out, seen.more(act_out))
            step(dve.scalar_tensor_tensor(gla_z, gla_z, 0.0, gla_t, ALU.min, ALU.subtract))
            flat = "p h t -> p (h t)"
            step(dve.tensor_tensor_scan(gla_b.rearrange(flat), gla_carry.rearrange(flat),
                                        gla_z.rearrange(flat), 0.0, ALU.mult, ALU.add))
            by_chunk = "p h (n c) -> p (h n) c"
            b_c = gla_b.rearrange(by_chunk, c=CHUNK)
            n_c = GH * T // CHUNK
            dve.tensor_tensor(gla_t.rearrange(by_chunk, c=CHUNK),
                              b_c[:, :, CHUNK - 1:CHUNK].broadcast_to([P, n_c, CHUNK]), b_c,
                              ALU.subtract).then_inc(for_act, 1)
            dve.wait_ge(act_out, seen.more(act_out))
            step(dve.tensor_tensor(gla_kend, gla_k, gla_kend, ALU.mult))
            dve.tensor_tensor(gla_k, gla_k, gla_z, ALU.mult)
            settle()
            dve.memset(gla_kt, 0.0)
            dve.memset(gla_scores, 0.0)
            dve.scalar_tensor_tensor(gla_q, gla_q, GDK ** -0.5, gla_eb, ALU.mult, ALU.mult).then_inc(for_pe, 1)
            dve.wait_ge(pe_out, seen.more(pe_out))
            for half in range(2):
                r = slice(half * CHUNK, (half + 1) * CHUNK)
                for tt in range(TT):
                    dve.tensor_copy(gla_kt[r, tt, :, half, :],
                                    psd[r, 2 + tt, :].rearrange("p (h d) -> p h d", h=GH))
            mark(for_pe)
            dve.wait_ge(pe_out, seen.more(pe_out))
            keep = const("same_chunk").bitcast(I32).unsqueeze(1).broadcast_to([P, 4, P])
            for b in range(2):
                dve.copy_predicated(gla_scores[:, 4 * b:4 * b + 4, :], keep,
                                    psa[:, b, :].rearrange("p (a t) -> p a t", a=4))
            mark(for_pe)
            for i in range(GH):
                dve.wait_ge(pe_out, seen.more(pe_out))
                b0 = 2 * (i % 2)
                kv = [psd[:, b0, 0:GDV], psd[:, b0, GDV:2 * GDV], psd[:, b0 + 1, 0:GDV]]
                step(dve.tensor_copy(gla_state[:, i, 0, :], kv[0]))
                for n in (1, 2):
                    decay = gla_eb[:, i, (n + 1) * CHUNK - 1:(n + 1) * CHUNK]
                    ins = dve.scalar_tensor_tensor(gla_state[:, i, n, :], gla_state[:, i, n - 1, :], decay,
                                                   kv[n], ALU.mult, ALU.add)
                    if n == 1:
                        step(ins)
                ins.then_inc(for_pe, 1)
            dve.wait_ge(pe_out, seen.more(pe_out))
            dve.tensor_copy(x32[:], psa[:].rearrange("p a (b t) -> p (a b) t", b=2)).then_inc(for_act, 1)
            dve.wait_ge(rstd_ready, seen.more(rstd_ready))
            dve.wait_ge(gate_out, seen.more(gate_out, 4))
            for k in range(KD):
                ins = dve.scalar_tensor_tensor(x32[:, k, :], x32[:, k, :], small("gla_g")[:, k % 2:k % 2 + 1],
                                               gla_rs[:, k // 2, :], ALU.mult, ALU.mult)
            step(ins)
            dve.tensor_tensor(x32[:], x32[:], gla_r, ALU.mult).then_inc(x32_ready, 1)
            split_x(WHOLE, x32, y_hi, y_lo)

            def scaled_residual(j):
                hj = h[:, 2 * j:2 * j + 2, :]
                return dve.scalar_tensor_tensor(hj, hj, ALPHA, pair(j), ALU.mult, ALU.add)
            units(4, scaled_residual, last=norm_in)
            layer_norm(0)

            def beats(score, n, n_x):
                def at(t, mine):
                    v = t[:, 0:n_x * EG].rearrange("p (x e) -> p x e", e=EG)
                    v = v.unsqueeze(3) if mine else v.unsqueeze(2)
                    return v.broadcast_to([P, n_x, EG, EG])
                full = slice(0, n_x * EG * EG)
                gt, ge = (t[:, full].rearrange("p (x j i) -> p x j i", j=EG, i=EG) for t in (r_gt, r_ge))
                dve.tensor_tensor(gt, at(score, False), at(score, True), ALU.is_gt)
                step(dve.tensor_tensor(ge, at(score, False), at(score, True), ALU.is_ge))
                step(dve.tensor_tensor(r_ge[:, full], r_ge[:, full], r_gt[:, full], ALU.subtract))
                lower = const("lower").unsqueeze(1).broadcast_to([P, n_x, EG * EG])
                g3 = r_ge[:, full].rearrange("p (x m) -> p x m", m=EG * EG)
                step(dve.tensor_tensor(g3, g3, lower, ALU.mult))
                step(dve.tensor_tensor(r_gt[:, full], r_gt[:, full], r_ge[:, full], ALU.add))
                step(dve.tensor_reduce(r_rank[:, 0:n_x * EG],
                                       r_gt[:, full].rearrange("p (x i) -> p x i", i=EG), AX.X, ALU.add))

            def route():
                dve.wait_ge(act_out, seen.more(act_out))
                by_token = "p (a e) -> p a e"
                bias = small("b_router").unsqueeze(1).broadcast_to([P, TT, NE])
                step(dve.tensor_tensor(r_b.rearrange(by_token, a=TT), r_s.rearrange(by_token, a=TT), bias, ALU.add))
                beats(r_b, TT * NE, TT * NE // EG)
                step(dve.tensor_scalar(r_sel, r_rank, 2.0, None, ALU.is_lt))
                step(dve.tensor_tensor(r_tmp, r_b, r_sel, ALU.mult))
                step(dve.tensor_reduce(r_grp, r_tmp.rearrange("p (x e) -> p x e", e=EG), AX.X, ALU.add))
                beats(r_grp, TT * EG, TT)
                step(dve.tensor_scalar(r_win, r_rank[:, 0:TT * EG], 1.0, None, ALU.is_lt))
                x_e = "p (x e) -> p x e"
                step(dve.tensor_tensor(r_sel.rearrange(x_e, e=EG), r_sel.rearrange(x_e, e=EG),
                                       r_win.unsqueeze(2).broadcast_to([P, TT * EG, EG]), ALU.mult))
                step(dve.tensor_tensor(r_sel, r_sel, r_s, ALU.mult))
                step(dve.tensor_reduce(r_den, r_sel.rearrange(by_token, a=TT), AX.X, ALU.add))
                step(dve.reciprocal(r_den, r_den))
                step(dve.memset(gate_pad, 0.0))
                dve.tensor_tensor(gate_pad[:, :, 0:NE], r_sel.rearrange(by_token, a=TT),
                                  r_den.unsqueeze(2).broadcast_to([P, TT, NE]), ALU.mult).then_inc(for_pe, 1)
                dve.wait_ge(pe_out, seen.more(pe_out))
                step(dve.tensor_copy(gate_t, psd[:, 1, 0:T]))
                for e in range(NE):
                    ins = dve.tensor_scalar(gate_rows[:, e, :], gate_t, ident[:, e:e + 1], None, ALU.mult)
                ins.then_inc(for_pe, 1)
                for e in range(NE // 2):
                    dve.wait_ge(pe_out, seen.more(pe_out))
                    dve.tensor_copy(gate_rows[:, 2 * e:2 * e + 2, :],
                                    psd[:, e % 4, :].rearrange("p (a t) -> p a t", a=2)).then_inc(for_pe, 1)

            route()
            feed_forward("moe0", NE, gate_rows, ALPHA)
            layer_norm(1)

            units(4, copy_to(nsa_q))

            def shifted(kind):
                def after(j):
                    dst = nsa_c32[:, kind, 2 * j:2 * j + 2, :]
                    dve.tensor_copy(dst[0:DH, :, :], pair(2 * kind + j)[0:DH])
                    return dve.tensor_copy(dst[DH:P, :, 0:T - 1], pair(2 * kind + j)[DH:P, :, 1:T])
                return after
            dve.memset(nsa_v, 0.0)
            dve.memset(nsa_ks, 0.0)
            dve.memset(nsa_kw, 0.0)
            dve.memset(nsa_hidr, 0.0)
            dve.memset(nsa_vc, 0.0)
            dve.memset(nsa_kc, 0.0)
            units(2, shifted(0))
            units(2, shifted(1))
            mark(x32_ready)
            for a in range(2):
                dve.wait_ge(xh_ready, seen.more(xh_ready))
                dve.tensor_tensor(y_lo[:, 4 * a:4 * a + 4, 0:T - 1], nsa_c32[:, a, :, 0:T - 1],
                                  y_hi[:, 4 * a:4 * a + 4, 0:T - 1], ALU.subtract).then_inc(x_ready, 1)
            units(4, lambda j: dve.tensor_copy(nsa_k32[:, j // 2, 2 * (j % 2):2 * (j % 2) + 2, :], pair(j)))

            def values(j):
                if j == 0:
                    return None
                for tt in range(TT):
                    ins = dve.tensor_copy(nsa_v[:, :, tt, :, DH:2 * DH],
                                          psa[:, tt, :].rearrange("p (b g d) -> p b g d", b=2, g=NG))
                return ins
            units(2, values)

            def rope(dst, n, c, s, products):
                tmp = x32[:, 0:n, :]
                dve.wait_ge(pe_out, seen.more(pe_out))
                dve.tensor_tensor(tmp, dst, c.unsqueeze(1).broadcast_to([P, n, T]), ALU.mult)
                settle()
                step(dve.tensor_tensor(dst, products, s.unsqueeze(1).broadcast_to([P, n, T]), ALU.mult))
                return tmp

            eight = psa[:].rearrange("p a (b t) -> p (a b) t", b=2)
            mark(for_pe)
            tmp = rope(nsa_q, KD, const("cosk"), const("sink"), eight)
            step(dve.tensor_tensor(nsa_q, nsa_q, tmp, ALU.add))
            mark(for_pe)
            both = nsa_k32.rearrange("p a g t -> p (a g) t")
            tmp = rope(both, KD, const("cosk"), const("sink"), eight)
            for half in range(2):
                r = slice(half * DH, (half + 1) * DH)
                dve.tensor_tensor(nsa_ks[r, :, half, :], both[r, 0:NG, :], tmp[r, 0:NG, :], ALU.add)
                dve.tensor_tensor(nsa_kw[r, :, half, :], both[r, NG:, :], tmp[r, NG:, :], ALU.add)
            mark(for_pe)
            for j in range(4):
                split_lo()
                dve.wait_ge(unit_done, seen.more(unit_done, tag="result"))
                step(dve.tensor_copy(stats[:, 32 + j:33 + j], psa[:, j, 60:61]))
                dve.tensor_scalar(nsa_hid[:, j, :], psa[:, j, 0:60], stats[:, 32 + j:33 + j], None,
                                  ALU.add).then_inc(for_act, 1)
            dve.wait_ge(act_out, seen.more(act_out, 1 + 4))
            for k in range(2):
                src = nsa_hid[:, 2 + k, :].rearrange("p (c g) -> p g c", g=NG).unsqueeze(2)
                ins = dve.tensor_copy(nsa_hidr[:, k].rearrange("p g (r c) -> p g r c", r=4)[:, :, :, 0:NCMP],
                                      src.broadcast_to([P, NG, 4, NCMP]))
            ins.then_inc(for_pe, 1)
            dve.wait_ge(pe_out, seen.more(pe_out))
            dve.tensor_copy(nsa_kcm[:, 0:60], psd[:, 0, 0:60]).then_inc(for_pe, 1)
            for j in range(2):
                for s in range(2):
                    r = slice(32 * (2 * j + s), 32 * (2 * j + s) + 32)
                    dve.tensor_copy(nsa_vc[r, :, j, DH * s:DH * s + DH],
                                    psd[r, 1, 0:NG * DH].rearrange("p (g d) -> p g d", g=NG))
            dve.wait_ge(pe_out, seen.more(pe_out))
            dve.tensor_tensor(nsa_kct[:, 0:60], psd[:, 2, 0:60], const("sinc"), ALU.mult)
            step(dve.tensor_tensor(nsa_kcm[:, 0:60], nsa_kcm[:, 0:60], const("cosc"), ALU.mult))
            for half in range(2):
                r = slice(half * DH, (half + 1) * DH)
                three = "p (c g) -> p g c"
                dve.tensor_tensor(nsa_kc[r, :, half, 0:NCMP], nsa_kcm[r, 0:60].rearrange(three, g=NG),
                                  nsa_kct[r, 0:60].rearrange(three, g=NG), ALU.add)
            mark(for_pe)
            dve.wait_ge(pe_out, seen.more(pe_out))
            for tt in range(TT):
                cm = const("cmask")[:, 32 * tt:32 * tt + 32].unsqueeze(1).broadcast_to([P, NHEADS, 32])
                ins = dve.tensor_tensor(nsa_s[:, tt], psd[:, tt, :].rearrange("p (h c) -> p h c", c=32), cm, ALU.add)
            step(ins)
            rows_s = nsa_s.rearrange("p a h c -> p (a h) c")
            rows_p = nsa_p.rearrange("p a h c -> p (a h) c")
            nrow = TT * NHEADS
            top, total, share = (nsa_st[:, i, :] for i in range(3))
            step(dve.tensor_reduce(top, rows_s, AX.X, ALU.max))
            dve.tensor_tensor(rows_s, rows_s, top.unsqueeze(2).broadcast_to([P, nrow, 32]),
                              ALU.subtract).then_inc(for_act, 1)
            dve.wait_ge(act_out, seen.more(act_out))
            step(dve.tensor_reduce(total, rows_p, AX.X, ALU.add))
            step(dve.reciprocal(share, total))
            by_head = "p (a h) -> p a h"
            g_c = nsa_gates.rearrange("p a (h r) -> p a h r", r=3)
            step(dve.tensor_tensor(share.rearrange(by_head, a=TT), share.rearrange(by_head, a=TT),
                                   g_c[:, :, :, 0], ALU.mult))
            step(dve.tensor_tensor(share.rearrange(by_head, a=TT), share.rearrange(by_head, a=TT),
                                   const("any_key").unsqueeze(2).broadcast_to([P, TT, NHEADS]), ALU.mult))
            dve.tensor_tensor(rows_p, rows_p, share.unsqueeze(2).broadcast_to([P, nrow, 32]),
                              ALU.mult).then_inc(for_pe, 1)
            dve.wait_ge(pe_out, seen.more(pe_out))
            dve.tensor_copy(nsa_pt, psd[:, 2:4, :].rearrange("p a (b t) -> p (a b) t", b=2)).then_inc(for_pe, 1)

            def branch_gate(t):
                head, branch = t // 2, t % 2
                return g_c[:, :, head, 1 + branch]
            attention(2 * NHEADS, DH ** -0.5, const("causal"), nsa_probs, nsa_probs_t,
                      lambda i: dve.tensor_copy(nsa_q[:, i, :], psd[:, 3, 0:T]), branch_gate, per_out=4)
            mark(x32_ready)
            split_x(WHOLE, nsa_q, y_hi, y_lo)
            units(4, scaled_residual, last=norm_in)
            layer_norm(2)
            route()
            feed_forward("moe1", NE, gate_rows, ALPHA, last=True)
            layer_norm(3, split=False)

        @block.tensor
        def _(pe):
            seen = Seen("pe", per_trip)
            seen.more(lo_done, SLOTS)
            ring = [0]
            pending = []

            def take():
                s = ring[0] % SLOTS
                ring[0] += 1
                pe.wait_ge(lo_done, seen.more(lo_done))
                return s

            def settle(leave=0):
                while len(pending) > leave:
                    signal = pending.pop(0)
                    pe.wait_ge(signal, seen.more(signal))

            def product(out, w, x, first, last, weights_move=False):
                (wh, wl), (xh, xl) = w, x
                for n, (a, b) in enumerate(((wh, xh), (wh, xl), (wl, xh))):
                    lhs, rhs = (b, a) if weights_move else (a, b)
                    ins = pe.matmul(out, lhs, rhs, start=first and n == 0, stop=last and n == 2,
                                    skip_group_check=True)
                return ins

            def parts(s, a, b):
                return w_hi[:, s, a:b], w_lo[:, s, a:b]

            def columns(outs, nk, x, k0=0, first_wait=()):
                s = take()
                n = len(outs)
                for j, out in enumerate(outs):
                    for k in range(nk):
                        if j == 0 and k in first_wait:
                            pe.wait_ge(x_ready, seen.more(x_ready))
                        c = (k * n + j) * P
                        ins = product(out, parts(s, c, c + P), (x[0][:, k0 + k, :], x[1][:, k0 + k, :]),
                                      k == 0, k == nk - 1)
                ins.then_inc(unit_done, 1)

            def block_of(b):
                return psa[:, b // 2, (b % 2) * T:(b % 2) * T + T]

            x, y = (x_hi, x_lo), (y_hi, y_lo)

            def dense(n, nk, blocks, operand, signal=evac, last=None, first_wait=(), k0=0, bank=0):
                banks = max(1, blocks // 2)
                for j in range(n):
                    settle(4 // banks - 1)
                    b0 = 2 * ((bank + j * banks) % 4)
                    columns([block_of(b0 + i) for i in range(blocks)], nk, operand, k0,
                            first_wait if j == 0 else ())
                    if last is None or j < n - 1:
                        pending.append(signal)

            def stat(n, src, signal=stat_done, out=None):
                for k in range(n):
                    ins = pe.matmul(psa[:, 3, 0:T] if out is None else out, ones, src[:, k, :],
                                    start=k == 0, stop=k == n - 1)
                ins.then_inc(signal, 1)

            def norm(n):
                settle()
                seen.more(norm_in)
                pe.wait_ge(sq_ready, seen.more(sq_ready))
                stat(n, x32)

            def layer_norm():
                settle()
                pe.wait_ge(norm_in, seen.more(norm_in))
                stat(KD, h, mean_done, psd[:, 0, 0:T])
                pe.wait_ge(sq_ready, seen.more(sq_ready))
                stat(KD, sq8)

            def feed_forward(label, trips, first_wait=(0, 4)):
                def gate_up(waits):
                    for bank in range(2):
                        columns([block_of(2 * bank), block_of(2 * bank + 1)], KD, x, 0, waits if bank == 0 else ())

                def down(last):
                    pe.wait_ge(hid_ready, seen.more(hid_ready))
                    s = take()
                    for k in range(2):
                        for b in range(KD):
                            c = k * D + b * P
                            out = psd[:, b // 2, (b % 2) * T:(b % 2) * T + T]
                            ins = product(out, parts(s, c, c + P), (y_hi[:, k, :], y_lo[:, k, :]),
                                          False, last and k == 1)
                    ins.then_inc(unit_done, 1)

                for b in range(4):
                    pe.matmul(psd[:, b, :], zero[:, 0:P], zero[:], start=True, stop=False, skip_group_check=True)
                gate_up(first_wait)
                with seen.loop(pe, label, trips - 1):
                    pe.wait_ge(side_ready, seen.more(side_ready))
                    gate_up(())
                    down(False)
                seen.more(side_ready)
                down(True)

            def attention(items, scores, lhs_v, probs, probs_t, per_out=1, before=None):
                def score(t):
                    if t >= 2:
                        pe.wait_ge(nmax_ready, seen.more(nmax_ready))
                    for tt in range(TT):
                        keys = P * (tt + 1)
                        out = psd[:, t % 2, P * tt:P * tt + keys]
                        terms = scores(t, tt, keys)
                        for n, (a, b) in enumerate(terms):
                            ins = pe.matmul(out, a, b, start=n == 0, stop=n == len(terms) - 1,
                                            skip_group_check=True)
                    ins.then_inc(s_done, 1)

                def turn(t):
                    pe.wait_ge(p_ready, seen.more(p_ready))
                    if t > 0:
                        pe.wait_ge(pt_ready, seen.more(pt_ready))
                    for i in range(3):
                        ins = pe.transpose(psd[:, 2, P * i:P * i + P], probs[:, t % 2, P * i:P * i + P], ident)
                    ins.then_inc(t_done, 1)

                def weigh(t):
                    if t == items - 1:
                        pe.wait_ge(pt_ready, seen.more(pt_ready))
                    first, last = t % per_out == 0, t % per_out == per_out - 1
                    if first and t > 0:
                        pe.wait_ge(o_done, seen.more(o_done))
                    opened = False
                    if first and before is not None:
                        pe.matmul(psd[:, 3, 0:T], *before(t // per_out), start=True, stop=False,
                                  skip_group_check=True)
                        opened = True
                    v0, v1 = lhs_v(t)
                    pe.matmul(psd[:, 3, 0:T], v0, probs_t[:, 0:T], start=first and not opened, stop=False,
                              skip_group_check=True)
                    pe.matmul(psd[:, 3, P:T], v1, probs_t[:, T:384], start=False, stop=last,
                              skip_group_check=True).then_inc(pv_done, 1)

                for t in range(items + 2):
                    if t < items:
                        score(t)
                    if 0 <= t - 1 < items:
                        turn(t - 1)
                    if 0 <= t - 2:
                        weigh(t - 2)
                seen.more(nmax_ready, 2)
                seen.more(o_done)

            pe.wait_ge(for_pe, seen.more(for_pe))
            with seen.loop(pe, "layers", DEPTH):
                norm(KD)
                feed_forward("ffn1", FF_TRIPS)
                norm(KD)
                for j, n in enumerate((2, 1, 2, 2)):
                    dense(1, KD, n, x, first_wait=(0, 4) if j == 0 else (), bank=j)
                dense(6, KD, 2, x)
                settle()
                dense(8, KD, 2, x, signal=gate_out)
                seen.more(x_ready)
                norm(3)
                norm(2)
                pe.wait_ge(x_ready, seen.more(x_ready, 2))
                dense(3, 3, 4, x)
                settle()
                dense(1, 2, KD, x, k0=3)
                settle()
                s = take()
                for tt in range(TT):
                    for half in range(2):
                        for k in range(2):
                            t0 = slice(tt * P, tt * P + P)
                            c = k * D + 512 * half
                            ins = product(psa[:, 2 * tt + half, :], parts(s, c, c + 512),
                                          (x_hi[:, 3 + k, t0], x_lo[:, 3 + k, t0]), k == 0, k == 1, True)
                ins.then_inc(unit_done, 1)
                pending.append(evac)
                settle()
                dense(2, 4, 4, y)

                def mla_scores(t, tt, keys):
                    q = slice(tt * P, tt * P + P)
                    return [(q_n[:, t, q], keys_n[:, t, 0:keys]),
                            (q_rot[:, t // 4, q], k_rot[:, 2 * (t % 4), 0:keys]),
                            (q_rot[:, 2 + t // 4, q], k_rot[:, 2 * (t % 4) + 1, 0:keys])]
                settle()
                attention(NH, mla_scores, lambda t: [vals[:, k, t * VD:t * VD + VD] for k in range(TT)],
                          probs1, probs_t1)
                dense(4, KD, 2, y, first_wait=(0,))
                settle()
                dense(4, KD, 2, x, last=norm_in, first_wait=(0,))
                norm(KD)
                feed_forward("ffn2", FF_TRIPS)
                norm(KD)
                pe.wait_ge(x_ready, seen.more(x_ready))
                dense(4, KD, 2, x, signal=gate_out, first_wait=(0, 4))
                settle()
                dense(2, 2, 4, y, last=norm_in)
                settle()
            norm(KD)

            dense(4, KD, 2, x, first_wait=(0, 4))
            settle()
            for m in range(4):
                s = take()
                for k in range(2):
                    kt = 2 * m + k
                    for tt in range(TT):
                        t0 = slice(tt * P, tt * P + P)
                        for half in range(2):
                            c = k * D + 512 * half
                            ins = product(psa[:, 2 * tt + half, :], parts(s, c, c + 512),
                                          (x_hi[:, kt, t0], x_lo[:, kt, t0]), kt == 0, kt == KD - 1, True)
                ins.then_inc(unit_done, 1)
            pending.append(evac)
            settle()
            dense(4, KD, 2, x, signal=gate_out)
            w_low = small("w_low").rearrange("p (k r) -> p k r", k=KD)
            for k in range(KD):
                ins = pe.matmul(psd[0:GRANK, 0, 0:T], w_low[:, k, :], h[:, k, :], start=k == 0, stop=k == KD - 1)
            ins.then_inc(pe_out, 1)
            pe.wait_ge(for_pe, seen.more(for_pe))
            for i in range(GH):
                ins = pe.matmul(psd[:, 1 + i // 2, (i % 2) * T:(i % 2) * T + T],
                                small("w_up")[0:GRANK, i * GDK:(i + 1) * GDK], gla_low[0:GRANK, :],
                                start=True, stop=True, skip_group_check=True)
            ins.then_inc(pe_out, 1)
            pe.wait_ge(for_pe, seen.more(for_pe))
            settle()
            for tt in range(TT):
                for i in range(GH):
                    ins = pe.transpose(psd[:, 2 + tt, P * i:P * i + P], gla_kend[:, i, tt * P:tt * P + P], ident)
            ins.then_inc(pe_out, 1)
            for i in range(GH):
                for tt in range(TT):
                    t0 = slice(tt * P, tt * P + P)
                    n = 2 * i + tt
                    ins = pe.matmul(psa[:, n // 4, (n % 4) * P:(n % 4) * P + P], gla_k[:, i, t0], gla_q[:, i, t0],
                                    start=True, stop=True, skip_group_check=True)
            ins.then_inc(pe_out, 1)
            pe.wait_ge(for_pe, seen.more(for_pe, 2))
            for i in range(GH):
                if i >= 2:
                    pe.wait_ge(for_pe, seen.more(for_pe))
                b0 = 2 * (i % 2)
                for n in range(3):
                    out = psd[:, b0 + n // 2, (n % 2) * GDV:(n % 2) * GDV + GDV]
                    ins = pe.matmul(out, gla_kt[:, n // 2, i, n % 2, :], gla_v[:, n // 2, i * GDV:(i + 1) * GDV],
                                    start=True, stop=True, skip_group_check=True)
                ins.then_inc(pe_out, 1)
            pe.wait_ge(for_pe, seen.more(for_pe, 2))
            for i in range(GH):
                for dv in range(2):
                    v0 = i * GDV + dv * P
                    for tt in range(TT):
                        pe.matmul(psa[:, i, dv * T + tt * P:dv * T + tt * P + P], gla_v[:, tt, v0:v0 + P],
                                  gla_scores[:, 2 * i + tt, :], start=dv == 0 and tt == 0, stop=False,
                                  skip_group_check=True)
                    for n in range(1, 4):
                        c = slice(n * CHUNK, (n + 1) * CHUNK)
                        ins = pe.matmul(psa[:, i, dv * T + n * CHUNK:dv * T + (n + 1) * CHUNK],
                                        gla_state[:, i, n - 1, dv * P:dv * P + P], gla_q[:, i, c],
                                        start=False, stop=dv == 1 and n == 3, skip_group_check=True)
            ins.then_inc(pe_out, 1)
            pe.wait_ge(sq_ready, seen.more(sq_ready))
            for i in range(GH):
                for k in range(2):
                    ins = pe.matmul(psd[:, i // 2, (i % 2) * T:(i % 2) * T + T], ones, sq8[:, 2 * i + k, :],
                                    start=k == 0, stop=k == 1, skip_group_check=True)
            ins.then_inc(stat_done, 1)
            dense(4, KD, 2, y, last=norm_in, first_wait=(0,))
            layer_norm()

            def route():
                w = small("w_router").rearrange("p (k e) -> p k e", k=KD)
                for tt in range(TT):
                    for k in range(KD):
                        ins = pe.matmul(psd[:, 0, tt * NE:(tt + 1) * NE], h[:, k, tt * P:tt * P + P], w[:, k, :],
                                        start=k == 0, stop=k == KD - 1, skip_group_check=True)
                ins.then_inc(pe_to_act, 1)
                pe.wait_ge(for_pe, seen.more(for_pe))
                for tt in range(TT):
                    ins = pe.transpose(psd[:, 1, tt * P:tt * P + P], gate_pad[:, tt, :], ident)
                ins.then_inc(pe_out, 1)
                pe.wait_ge(for_pe, seen.more(for_pe))
                for e in range(NE // 2):
                    if e >= 4:
                        pe.wait_ge(for_pe, seen.more(for_pe))
                    pe.matmul(psd[:, e % 4, :], ones, gate_rows[:, 2 * e:2 * e + 2, :],
                              start=True, stop=True).then_inc(pe_out, 1)
                pe.wait_ge(for_pe, seen.more(for_pe, 4))

            pe.wait_ge(x_ready, seen.more(x_ready, 2))
            route()
            feed_forward("moe0", NE, ())
            layer_norm()

            dense(4 + 4, KD, 2, x, first_wait=(0, 4))
            dense(4, KD, 2, x)
            settle()
            for m in range(2):
                s = take()
                for k in range(4):
                    kt = 4 * m + k
                    for tt in range(TT):
                        t0 = slice(tt * P, tt * P + P)
                        ins = product(psa[:, tt, :], parts(s, 512 * k, 512 * k + 512),
                                      (x_hi[:, kt, t0], x_lo[:, kt, t0]), kt == 0, kt == KD - 1, True)
                ins.then_inc(unit_done, 1)
            pending.append(evac)
            w_gates = small("w_gates").rearrange("p (k c) -> p k c", k=KD)
            for tt in range(TT):
                for k in range(KD):
                    ins = pe.matmul(psd[:, 0, tt * 48:(tt + 1) * 48], h[:, k, tt * P:tt * P + P], w_gates[:, k, :],
                                    start=k == 0, stop=k == KD - 1, skip_group_check=True)
            ins.then_inc(pe_to_act, 1)
            settle()
            for src in (nsa_q, nsa_k32.rearrange("p a g t -> p (a g) t")):
                pe.wait_ge(for_pe, seen.more(for_pe))
                for b in range(4):
                    ins = pe.matmul(psa[:, b, :], const("rot"), src[:, 2 * b:2 * b + 2, :], start=True, stop=True)
                ins.then_inc(pe_out, 1)
            pe.wait_ge(for_pe, seen.more(for_pe))
            pe.wait_ge(x_ready, seen.more(x_ready, 2))
            for j in range(4):
                s = take()
                kind = j // 2
                c_hi, c_lo = y_hi[:, 4 * kind:4 * kind + 4, :], y_lo[:, 4 * kind:4 * kind + 4, :]
                for i in range(16):
                    t0 = slice(2 * i, 2 * i + CSTR * (NCMP - 1) + 1, CSTR)
                    out = psa[:, j, 0:60].rearrange("p (c g) -> p c g", g=NG)
                    by_block = [c[:, :, t0].rearrange("p g c -> p c g") for c in (c_hi, c_lo)]
                    product(out, parts(s, i * P, i * P + P), by_block, i == 0, False)
                    ins = product(psa[:, j, 60:62], parts(s, i * P, i * P + P),
                                  (pe_hi[:, 2 * i:2 * i + 2], pe_lo[:, 2 * i:2 * i + 2]), False, i == 15)
                ins.then_inc(unit_done, 1)
            pe.wait_ge(for_pe, seen.more(for_pe))
            w2k = small("w2k").rearrange("p (k c) -> p k c", k=2)
            w2v = small("w2v").rearrange("p (k c) -> p k c", k=2)
            for k in range(2):
                pe.matmul(psd[:, 0, 0:60], w2k[:, k, :], nsa_hid[:, k, :], start=k == 0, stop=k == 1)
            for gr in range(NG):
                for k in range(2):
                    ins = pe.matmul(psd[:, 1, gr * DH:(gr + 1) * DH], nsa_hidr[:, k, gr, :], w2v[:, k, :],
                                    start=k == 0, stop=k == 1, skip_group_check=True)
            ins.then_inc(pe_out, 1)
            pe.wait_ge(for_pe, seen.more(for_pe))
            pe.matmul(psd[:, 2, 0:60], const("rot"), nsa_kcm[:, 0:60], start=True, stop=True).then_inc(pe_out, 1)
            pe.wait_ge(for_pe, seen.more(for_pe))
            for tt in range(TT):
                for j in range(KD):
                    ins = pe.matmul(psd[:, tt, 64 * j:64 * j + 64], nsa_q[:, j, tt * P:tt * P + P],
                                    nsa_kc[:, j // 2].rearrange("p a c -> p (a c)"),
                                    start=True, stop=True, skip_group_check=True)
            ins.then_inc(pe_out, 1)
            pe.wait_ge(for_pe, seen.more(for_pe))
            for gr in range(NG):
                for tt in range(TT):
                    ins = pe.transpose(psd[:, 2 + gr // 2, (gr % 2) * T + tt * P:(gr % 2) * T + tt * P + P],
                                       nsa_p[:, tt, 4 * gr:4 * gr + 4, :].rearrange("p a c -> p (a c)"), ident)
            ins.then_inc(pe_out, 1)
            pe.wait_ge(for_pe, seen.more(for_pe))

            def nsa_scores(t, tt, keys):
                head, branch = t // 2, t % 2
                k = (nsa_ks, nsa_kw)[branch]
                return [(nsa_q[:, head // 2, tt * P:tt * P + P], k[:, head // HPG, head % 2, 0:keys])]

            def nsa_values(t):
                head, branch = t // 2, t % 2
                c = DH if head % 2 == 0 else 0
                return [nsa_v[:, branch, k, head // HPG, c:c + P] for k in range(TT)]
            attention(2 * NHEADS, nsa_scores, nsa_values, nsa_probs, nsa_probs_t, 4,
                      lambda j: (nsa_vc[:, j // 2, j % 2, :], nsa_pt[:, j // 2, :]))
            dense(4, KD, 2, y, last=norm_in, first_wait=(0,))
            layer_norm()
            pe.wait_ge(x_ready, seen.more(x_ready, 2))
            route()
            feed_forward("moe1", NE, ())
            layer_norm()


def kernel(**inputs):
    import concourse.bacc as bacc
    from concourse.bass_utils import run_bass_kernel_spmd

    a = {name: np.asarray(v) for name, v in inputs.items()}

    def by_feature(m):
        return np.ascontiguousarray(rows(np.ascontiguousarray(m.T)))

    arrays = {
        "weights": weight_stream(a),
        "consts": constants(),
        "smalls": small_operands(a),
        "x_in": by_feature(a["x"][0]),
        "p_in": np.concatenate([by_feature(a["p"][l, 0]) for l in range(DEPTH)], 1),
        "pos_in": np.ascontiguousarray(np.broadcast_to(a["positions"][0][None], (P, T))),
    }

    def program(per_trip):
        nc = bacc.Bacc("TRN2", target_bir_lowering=False, num_devices=1)
        aps = [nc.dram_tensor(n, v.shape, mybir.dt.from_np(v.dtype), kind="ExternalInput").ap()
               for n, v in arrays.items()]
        out = nc.dram_tensor("result", (P, KD, T), F32, kind="ExternalOutput").ap()
        two_blocks(nc, per_trip, *aps, out)
        return nc

    per_trip = {}
    program(per_trip)
    nc = program(per_trip)
    r = run_bass_kernel_spmd(nc, [arrays], core_ids=[0])
    res = r.results[0]["result"]
    return np.ascontiguousarray(res.transpose(1, 0, 2).reshape(D, T).T)[None]
```
